# Optimizing a Trainium2 kernel written in Bass

```python
import math
import jax, jax.numpy as jnp
from jax import lax
import numpy as np

D_MODEL = 1024
BATCH = 1
SEQ = 256
DEPTH = 2

HEAD_DIM = 64
N_RET = 6
N_NSA = 6
N_KV = 2
HPG = N_NSA // N_KV
N_GM = 4
GM_DIM = 64
RET_W = N_RET * HEAD_DIM
NSA_W = N_NSA * HEAD_DIM
GM_W = N_GM * GM_DIM
MIX_W = RET_W + NSA_W + GM_W
RET_CHUNK = 128
CMP_LEN = 32
CMP_STRIDE = 16
SEL_BLOCK = 64
N_SEL = 16
WINDOW = 512
Q_BLOCK = 128
GM_CHUNK = 128
N_BUCKETS = 32
MAX_DISTANCE = 128
ROPE_THETA = 10000.0
D_FF = -(-8 * D_MODEL // (3 * 256)) * 256
SPLIT_SIZES = (RET_W, RET_W, RET_W, RET_W, NSA_W, 3 * 2 * N_KV * HEAD_DIM, 3 * N_NSA, 2 * GM_W)
IN_W = sum(SPLIT_SIZES)
EPS = 1e-6
BIG = 1e9
NEG = -1e30


def rms_norm(x, gain=None):
    xf = x.astype(jnp.float32)
    y = xf * lax.rsqrt(jnp.mean(xf * xf, axis=-1, keepdims=True) + EPS)
    if gain is not None:
        y = y * gain.astype(jnp.float32)
    return y.astype(x.dtype)

def rope(x, pos):
    half = x.shape[-1] // 2
    inv = ROPE_THETA ** (-jnp.arange(half, dtype=jnp.float32) / half)
    ang = pos.astype(jnp.float32)[:, None] * inv[None, :]
    cos = jnp.cos(ang)[None, :, None, :]
    sin = jnp.sin(ang)[None, :, None, :]
    x1 = x[..., :half].astype(jnp.float32)
    x2 = x[..., half:].astype(jnp.float32)
    return jnp.concatenate([x1 * cos - x2 * sin, x2 * cos + x1 * sin], axis=-1).astype(x.dtype)

def t5_bucket(dist):
    n = jnp.maximum(dist, 0)
    max_exact = N_BUCKETS // 2
    nf = jnp.maximum(n, 1).astype(jnp.float32)
    large = max_exact + (jnp.log(nf / max_exact) / math.log(MAX_DISTANCE / max_exact)
                         * (N_BUCKETS - max_exact)).astype(jnp.int32)
    large = jnp.minimum(large, N_BUCKETS - 1)
    return jnp.where(n < max_exact, n, large)

def masked_softmax(logits, mask):
    s = jnp.where(mask, logits.astype(jnp.float32), NEG)
    return jax.nn.softmax(s, axis=-1) * mask

def retention(q, k, v, g):
    B, T, H, d = q.shape
    C = RET_CHUNK
    nc = T // C
    f32 = jnp.float32
    to_chunks = lambda a: a.astype(f32).reshape(B, nc, C, H, d).transpose(0, 3, 1, 2, 4)
    qc, kc, vc = to_chunks(q), to_chunks(k * d ** -0.5), to_chunks(v)
    log_gamma = jnp.log(1.0 - 2.0 ** (-5.0 - jnp.arange(H, dtype=f32)))
    idx = jnp.arange(C, dtype=f32)
    diff = idx[:, None] - idx[None, :]
    decay = jnp.where(diff >= 0, jnp.exp(jnp.maximum(diff, 0.0)[None] * log_gamma[:, None, None]), 0.0)
    scores = jnp.einsum('bhcnd,bhcmd->bhcnm', qc, kc) * decay[:, None]
    inner = jnp.einsum('bhcnm,bhcme->bhcne', scores, vc)
    zeta = jnp.exp((C - 1 - idx)[None, :] * log_gamma[:, None])
    xi = jnp.exp((idx + 1)[None, :] * log_gamma[:, None])
    chunk_decay = jnp.exp(C * log_gamma)

    def step(R, kv):
        kt, vt = kv
        R_new = chunk_decay[None, :, None, None] * R + jnp.einsum('bhmd,bhme->bhde', kt * zeta[None, :, :, None], vt)
        return R_new, R

    R0 = jnp.zeros((B, H, d, d), f32)
    _, R_prev = lax.scan(step, R0, (kc.transpose(2, 0, 1, 3, 4), vc.transpose(2, 0, 1, 3, 4)))
    cross = jnp.einsum('bhcnd,cbhde->bhcne', qc, R_prev) * xi[None, :, None, :, None]
    o = (inner + cross).transpose(0, 2, 3, 1, 4).reshape(B, T, H, d)
    o = rms_norm(o) * jax.nn.silu(g.astype(f32))
    return o.reshape(B, T, H * d).astype(q.dtype)

def nsa(q, kv, gates, q_gain, k_gain, cmp_pe, cmp_w1, cmp_w2, rel_bias):
    B, T, _, d = q.shape
    out_dtype = q.dtype
    q = rms_norm(q, q_gain) * d ** -0.5
    q = q.reshape(B, T, N_KV, HPG, d).transpose(0, 2, 3, 1, 4)
    kv = kv.transpose(2, 3, 0, 4, 1, 5)

    n_cmp = (T - CMP_LEN) // CMP_STRIDE + 1
    blk_idx = np.arange(n_cmp)[:, None] * CMP_STRIDE + np.arange(CMP_LEN)[None, :]

    def compress(a, j):
        blocks = a[:, :, blk_idx] + cmp_pe[j]
        flat = blocks.reshape(B, N_KV, n_cmp, CMP_LEN * d)
        return jax.nn.gelu(flat @ cmp_w1[j]) @ cmp_w2[j]

    k_cmp = rms_norm(compress(kv[0, 0], 0), k_gain[0])
    v_cmp = compress(kv[0, 1], 1)
    cmp_end = jnp.asarray(blk_idx[:, -1], jnp.int32)

    n_slc = T // SEL_BLOCK
    n_sel = min(N_SEL, n_slc)
    k_sel = rms_norm(kv[1, 0], k_gain[1]).reshape(B, N_KV, n_slc, SEL_BLOCK, d)
    v_sel = kv[1, 1].reshape(B, N_KV, n_slc, SEL_BLOCK, d)
    cs = np.arange(n_cmp)[:, None] * CMP_STRIDE
    ss = np.arange(n_slc)[None, :] * SEL_BLOCK
    overlap = np.clip(np.minimum(cs + CMP_LEN, ss + SEL_BLOCK) - np.maximum(cs, ss), 0, None) // CMP_STRIDE
    overlap = jnp.asarray(overlap, jnp.float32)

    pad = ((0, 0), (0, 0), (WINDOW, 0), (0, 0))
    k_win = jnp.pad(rms_norm(kv[2, 0], k_gain[2]), pad)
    v_win = jnp.pad(kv[2, 1], pad)

    gates_t = jax.nn.sigmoid(gates.astype(jnp.float32)).reshape(B, T, N_KV, HPG, 3).transpose(0, 2, 3, 1, 4)
    bias_tab = rel_bias.reshape(N_BUCKETS, N_KV, HPG)
    bi = jnp.arange(B)[:, None, None, None]
    gi = jnp.arange(N_KV)[None, :, None, None]
    K_SEL = n_sel * SEL_BLOCK

    def block(i):
        q0 = i * Q_BLOCK
        qb = lax.dynamic_slice_in_dim(q, q0, Q_BLOCK, axis=3)
        t = q0 + jnp.arange(Q_BLOCK, dtype=jnp.int32)

        dist_c = t[:, None] - cmp_end[None, :]
        bias_c = bias_tab[t5_bucket(dist_c)].transpose(2, 3, 0, 1)
        s_c = jnp.einsum('bghqd,bgnd->bghqn', qb, k_cmp) + bias_c
        p_c = masked_softmax(s_c, dist_c >= 0)
        o_c = jnp.einsum('bghqn,bgnd->bghqd', p_c, v_cmp)

        imp = jnp.einsum('bghqn,nj->bgqj', p_c, overlap)
        cur = (t // SEL_BLOCK)[:, None]
        j = jnp.arange(n_slc)[None, :]
        imp = jnp.where((j == 0) | (j == cur) | (j == cur - 1), BIG, imp)
        imp = jnp.where(j > cur, -BIG, imp)
        _, sel = lax.top_k(imp, n_sel)
        ks = k_sel[bi, gi, sel].reshape(B, N_KV, Q_BLOCK, K_SEL, d)
        vs = v_sel[bi, gi, sel].reshape(B, N_KV, Q_BLOCK, K_SEL, d)
        pos = sel[..., None] * SEL_BLOCK + jnp.arange(SEL_BLOCK, dtype=jnp.int32)
        dist_s = (t[None, None, :, None, None] - pos).reshape(B, N_KV, Q_BLOCK, K_SEL)
        bias_s = bias_tab[t5_bucket(dist_s), gi].transpose(0, 1, 4, 2, 3)
        s_s = jnp.einsum('bghqd,bgqkd->bghqk', qb, ks) + bias_s
        p_s = masked_softmax(s_s, (dist_s >= 0)[:, :, None])
        o_s = jnp.einsum('bghqk,bgqkd->bghqd', p_s, vs)

        kw = lax.dynamic_slice_in_dim(k_win, q0, WINDOW + Q_BLOCK, axis=2)
        vw = lax.dynamic_slice_in_dim(v_win, q0, WINDOW + Q_BLOCK, axis=2)
        s_pos = q0 - WINDOW + jnp.arange(WINDOW + Q_BLOCK, dtype=jnp.int32)
        dist_w = t[:, None] - s_pos[None, :]
        mask_w = (dist_w >= 0) & (dist_w < WINDOW) & (s_pos[None, :] >= 0)
        bias_w = bias_tab[t5_bucket(dist_w)].transpose(2, 3, 0, 1)
        s_w = jnp.einsum('bghqd,bgkd->bghqk', qb, kw) + bias_w
        p_w = masked_softmax(s_w, mask_w)
        o_w = jnp.einsum('bghqk,bgkd->bghqd', p_w, vw)

        g = lax.dynamic_slice_in_dim(gates_t, q0, Q_BLOCK, axis=3)
        return g[..., 0:1] * o_c + g[..., 1:2] * o_s + g[..., 2:3] * o_w

    out = lax.map(block, jnp.arange(T // Q_BLOCK, dtype=jnp.int32))
    return out.transpose(1, 0, 4, 2, 3, 5).reshape(B, T, N_NSA * d).astype(out_dtype)

def spatial_gating(z, ws, b):
    B, T, _ = z.shape
    nch = T // GM_CHUNK
    z = jax.nn.gelu(z)
    u, v = jnp.split(z, 2, axis=-1)
    v = rms_norm(v.reshape(B, nch, GM_CHUNK, N_GM, GM_DIM))
    causal = jnp.tril(jnp.ones((GM_CHUNK, GM_CHUNK), ws.dtype))
    sv = jnp.einsum('gts,bcsgd->bctgd', ws * causal, v) + b.T[None, None, :, :, None]
    return (u.reshape(B, nch, GM_CHUNK, N_GM, GM_DIM) * sv).reshape(B, T, GM_W)

def first_inputs(seed: int = 0) -> dict:
    key = jax.random.key(seed)
    ks = jax.random.split(key, 16)
    f32 = jnp.float32
    nrm = lambda k, shape, scale: jax.random.normal(k, shape, f32) * scale
    return {
        "x": nrm(ks[0], (BATCH, SEQ, D_MODEL), 1.0),
        "attn_norm": 1.0 + nrm(ks[1], (DEPTH, D_MODEL), 0.02),
        "w_in": nrm(ks[2], (DEPTH, D_MODEL, IN_W), D_MODEL ** -0.5),
        "w_out": nrm(ks[3], (DEPTH, MIX_W, D_MODEL), MIX_W ** -0.5),
        "nsa_q_gain": 1.0 + nrm(ks[4], (DEPTH, HEAD_DIM), 0.02),
        "nsa_k_gain": 1.0 + nrm(ks[5], (DEPTH, 3, HEAD_DIM), 0.02),
        "cmp_pe": nrm(ks[6], (DEPTH, 2, CMP_LEN, HEAD_DIM), 0.1),
        "cmp_w1": nrm(ks[7], (DEPTH, 2, CMP_LEN * HEAD_DIM, HEAD_DIM), (CMP_LEN * HEAD_DIM) ** -0.5),
        "cmp_w2": nrm(ks[8], (DEPTH, 2, HEAD_DIM, HEAD_DIM), HEAD_DIM ** -0.5),
        "gm_ws": nrm(ks[9], (DEPTH, N_GM, GM_CHUNK, GM_CHUNK), GM_CHUNK ** -0.5),
        "gm_b": 1.0 + nrm(ks[10], (DEPTH, N_GM, GM_CHUNK), 0.02),
        "ffn_norm": 1.0 + nrm(ks[11], (DEPTH, D_MODEL), 0.02),
        "w_gate_up": nrm(ks[12], (DEPTH, D_MODEL, 2 * D_FF), D_MODEL ** -0.5),
        "w_down": nrm(ks[13], (DEPTH, D_FF, D_MODEL), D_FF ** -0.5),
        "rel_bias": nrm(ks[14], (N_BUCKETS, N_NSA), 0.5),
    }

def first_block(x, attn_norm, w_in, w_out, nsa_q_gain, nsa_k_gain, cmp_pe, cmp_w1, cmp_w2,
              gm_ws, gm_b, ffn_norm, w_gate_up, w_down, rel_bias):
    B, T, _ = x.shape
    pos = jnp.arange(T, dtype=jnp.int32)
    split_points = [int(s) for s in np.cumsum(SPLIT_SIZES)[:-1]]
    for l in range(DEPTH):
        h = rms_norm(x, attn_norm[l])
        proj = h @ w_in[l]
        r_q, r_k, r_v, r_g, n_q, n_kv, n_g, gm_z = jnp.split(proj, split_points, axis=-1)
        hs = (B, T, N_RET, HEAD_DIM)
        ret_o = retention(rope(r_q.reshape(hs), pos), rope(r_k.reshape(hs), pos),
                          r_v.reshape(hs), r_g.reshape(hs))
        nsa_o = nsa(n_q.reshape(B, T, N_NSA, HEAD_DIM),
                    n_kv.reshape(B, T, 3, 2, N_KV, HEAD_DIM),
                    n_g.reshape(B, T, N_NSA, 3),
                    nsa_q_gain[l], nsa_k_gain[l], cmp_pe[l], cmp_w1[l], cmp_w2[l], rel_bias)
        gm_o = spatial_gating(gm_z, gm_ws[l], gm_b[l])
        mix = jnp.concatenate([ret_o, nsa_o.astype(ret_o.dtype), gm_o.astype(ret_o.dtype)], axis=-1)
        x = x + (mix @ w_out[l]).astype(x.dtype)
        h = rms_norm(x, ffn_norm[l])
        gate, up = jnp.split(h @ w_gate_up[l], 2, axis=-1)
        x = x + ((jax.nn.silu(gate) * up) @ w_down[l]).astype(x.dtype)
    return x


DEPTH_2 = 1

D_MIX = D_MODEL
GLA_WIDTH = D_MIX // 2
S5_WIDTH = D_MIX - GLA_WIDTH
GLA_HEADS = 4
GLA_DV = GLA_WIDTH // GLA_HEADS
GLA_DK = GLA_DV // 2
GLA_LOWRANK = 16
GLA_TAU = 16.0
GLA_CHUNK = 64
S5_CH = 16
S5_GROUPS = S5_WIDTH // S5_CH
S5_STATE = 64
DT_MIN = 1e-3
DT_MAX = 1e-1
N_EXPERTS = 32
TOP_K = 4
D_FF_2 = D_MODEL
SWIGLU_ALPHA = 1.702
SWIGLU_LIMIT = 7.0
MOE_BLOCK = 128
Q_COLS = GLA_HEADS * GLA_DK
K_COLS = GLA_HEADS * GLA_DK
V_COLS = GLA_WIDTH
G_COLS = GLA_WIDTH
A_COLS = GLA_LOWRANK
U_COLS = S5_WIDTH
N_IN = Q_COLS + K_COLS + V_COLS + G_COLS + A_COLS + U_COLS
SPLITS = [Q_COLS, Q_COLS + K_COLS, Q_COLS + K_COLS + V_COLS, Q_COLS + K_COLS + V_COLS + G_COLS,
          Q_COLS + K_COLS + V_COLS + G_COLS + A_COLS]


def rmsnorm(x, g):
    xf = x.astype(jnp.float32)
    r = lax.rsqrt(jnp.mean(xf * xf, axis=-1, keepdims=True) + EPS)
    return (xf * r * g.astype(jnp.float32)).astype(x.dtype)

def gla_chunked(q, k, v, log_a):
    f32 = jnp.float32
    B_, H_, T_, DK_ = q.shape
    DV_ = v.shape[-1]
    C = GLA_CHUNK
    nc = T_ // C
    q = q.astype(f32).reshape(B_, H_, nc, C, DK_) * (DK_ ** -0.5)
    k = k.astype(f32).reshape(B_, H_, nc, C, DK_)
    v = v.astype(f32).reshape(B_, H_, nc, C, DV_)
    b = jnp.cumsum(log_a.astype(f32).reshape(B_, H_, nc, C, DK_), axis=3)
    b_last = b[:, :, :, -1:, :]
    q_dec = q * jnp.exp(b)
    k_inv = k * jnp.exp(-b)
    k_to_end = k * jnp.exp(b_last - b)
    causal = jnp.tril(jnp.ones((C, C), dtype=bool))
    scores = jnp.where(causal, jnp.einsum('bhnik,bhnjk->bhnij', q_dec, k_inv), 0.0)
    o_intra = jnp.einsum('bhnij,bhnjv->bhniv', scores, v)
    delta = jnp.einsum('bhnjk,bhnjv->bhnkv', k_to_end, v)
    decay = jnp.exp(b_last[:, :, :, 0, :])

    def step(S, inp):
        d, dS = inp
        return d[..., None] * S + dS, S

    S0 = jnp.zeros((B_, H_, DK_, DV_), f32)
    _, S_prev = lax.scan(step, S0, (jnp.moveaxis(decay, 2, 0), jnp.moveaxis(delta, 2, 0)))
    S_prev = jnp.moveaxis(S_prev, 0, 2)
    o_inter = jnp.einsum('bhnik,bhnkv->bhniv', q_dec, S_prev)
    return (o_intra + o_inter).reshape(B_, H_, T_, DV_)

def s5_layer(u, lam_re, lam_im, log_dt, b_re, b_im, c_re, c_im, d, glu_w, glu_b):
    f32 = jnp.float32
    B_, T_, _ = u.shape
    uf = u.astype(f32).reshape(B_, T_, S5_GROUPS, S5_CH)
    lr = lam_re.astype(f32)
    li = lam_im.astype(f32)
    dt = jnp.exp(log_dt.astype(f32))[:, None]
    mag = jnp.exp(lr * dt)
    ab_re = mag * jnp.cos(li * dt)
    ab_im = mag * jnp.sin(li * dt)
    den = lr * lr + li * li
    f_re = ((ab_re - 1.0) * lr + ab_im * li) / den
    f_im = (ab_im * lr - (ab_re - 1.0) * li) / den
    br = b_re.astype(f32)
    bi = b_im.astype(f32)
    bb_re = f_re[..., None] * br - f_im[..., None] * bi
    bb_im = f_re[..., None] * bi + f_im[..., None] * br
    bu_re = jnp.einsum('btgh,gph->btgp', uf, bb_re)
    bu_im = jnp.einsum('btgh,gph->btgp', uf, bb_im)
    a_re = jnp.broadcast_to(ab_re, (1, T_, S5_GROUPS, S5_STATE))
    a_im = jnp.broadcast_to(ab_im, (1, T_, S5_GROUPS, S5_STATE))

    def combine(e1, e2):
        a1r, a1i, b1r, b1i = e1
        a2r, a2i, b2r, b2i = e2
        return (a2r * a1r - a2i * a1i,
                a2r * a1i + a2i * a1r,
                a2r * b1r - a2i * b1i + b2r,
                a2r * b1i + a2i * b1r + b2i)

    _, _, xr, xi = lax.associative_scan(combine, (a_re, a_im, bu_re, bu_im), axis=1)
    y = (jnp.einsum('btgp,ghp->btgh', xr, c_re.astype(f32))
         - jnp.einsum('btgp,ghp->btgh', xi, c_im.astype(f32))
         + d.astype(f32) * uf)
    y = jax.nn.gelu(y.reshape(B_, T_, S5_WIDTH))
    return y * jax.nn.sigmoid(y @ glu_w.astype(f32) + glu_b.astype(f32))

def moe_ffn(h, router_w, router_b, w_gu, b_gu, w_down, b_down):
    f32 = jnp.float32
    B_, T_, D_ = h.shape
    N = B_ * T_
    NK = N * TOP_K
    xt = h.reshape(N, D_)
    logits = (xt @ router_w + router_b).astype(f32)
    top_val, top_idx = lax.top_k(logits, TOP_K)
    gate = jax.nn.softmax(top_val, axis=-1)
    flat_e = top_idx.reshape(NK).astype(jnp.int32)
    flat_tok = jnp.arange(NK, dtype=jnp.int32) // TOP_K
    flat_w = gate.reshape(NK)
    order = jnp.argsort(flat_e)
    se, stok, sw = flat_e[order], flat_tok[order], flat_w[order]
    counts = jnp.zeros((N_EXPERTS,), jnp.int32).at[flat_e].add(1)
    starts = jnp.cumsum(counts) - counts
    padded = (counts + MOE_BLOCK - 1) // MOE_BLOCK * MOE_BLOCK
    pends = jnp.cumsum(padded)
    pstarts = pends - padded
    dest = pstarts[se] + jnp.arange(NK, dtype=jnp.int32) - starts[se]
    n_blocks = -(-NK // MOE_BLOCK) + N_EXPERTS
    cap = n_blocks * MOE_BLOCK
    tok_buf = jnp.full((cap,), N, jnp.int32).at[dest].set(stok)
    w_buf = jnp.zeros((cap,), f32).at[dest].set(sw)
    block_e = jnp.minimum(
        jnp.searchsorted(pends, jnp.arange(n_blocks, dtype=jnp.int32) * MOE_BLOCK, side='right'),
        N_EXPERTS - 1).astype(jnp.int32)
    x_pad = jnp.concatenate([xt, jnp.zeros((1, D_), xt.dtype)], axis=0)
    xb = x_pad[tok_buf].reshape(n_blocks, MOE_BLOCK, D_)

    def expert_block(args):
        xblk, e = args
        gu = xblk @ w_gu[e] + b_gu[e]
        g, up = gu[:, :D_FF_2], gu[:, D_FF_2:]
        g = jnp.minimum(g, SWIGLU_LIMIT)
        up = jnp.clip(up, -SWIGLU_LIMIT, SWIGLU_LIMIT)
        act = (up + 1.0) * (g * jax.nn.sigmoid(SWIGLU_ALPHA * g))
        return act @ w_down[e] + b_down[e]

    yb = lax.map(expert_block, (xb, block_e)).reshape(cap, D_)
    out = jnp.zeros((N + 1, D_), f32).at[tok_buf].add(yb.astype(f32) * w_buf[:, None])[:N]
    return out.reshape(B_, T_, D_).astype(h.dtype)

def second_inputs(seed: int = 0) -> dict:
    key = jax.random.key(seed)
    ks = jax.random.split(key, 32)
    f32 = jnp.float32
    L, D = DEPTH_2, D_MODEL

    def nrm(k, shape, scale):
        return jax.random.normal(k, shape, f32) * scale

    n_idx = jnp.arange(S5_STATE, dtype=f32)
    return {
        "x": nrm(ks[0], (BATCH, SEQ, D), 1.0),
        "c": nrm(ks[1], (BATCH, D), 1.0),
        "ada_w": nrm(ks[2], (L, D, 6 * D), 0.02),
        "ada_b": nrm(ks[3], (L, 6 * D), 0.02),
        "mix_pre_g": 1.0 + nrm(ks[4], (L, D), 0.05),
        "mix_post_g": 1.0 + nrm(ks[5], (L, D), 0.05),
        "ffn_pre_g": 1.0 + nrm(ks[6], (L, D), 0.05),
        "ffn_post_g": 1.0 + nrm(ks[7], (L, D), 0.05),
        "w_in": nrm(ks[8], (L, D, N_IN), D ** -0.5),
        "w_alpha": nrm(ks[9], (L, GLA_LOWRANK, GLA_HEADS * GLA_DK), GLA_LOWRANK ** -0.5),
        "b_alpha": nrm(ks[10], (L, GLA_HEADS * GLA_DK), 0.1),
        "gla_norm_g": 1.0 + nrm(ks[11], (L, GLA_DV), 0.05),
        "s5_lambda_re": -0.5 + nrm(ks[12], (L, S5_GROUPS, S5_STATE), 0.01),
        "s5_lambda_im": math.pi * n_idx + nrm(ks[13], (L, S5_GROUPS, S5_STATE), 0.01),
        "s5_log_dt": jax.random.uniform(ks[14], (L, S5_GROUPS), f32, math.log(DT_MIN), math.log(DT_MAX)),
        "s5_b_re": nrm(ks[15], (L, S5_GROUPS, S5_STATE, S5_CH), (2 * S5_CH) ** -0.5),
        "s5_b_im": nrm(ks[16], (L, S5_GROUPS, S5_STATE, S5_CH), (2 * S5_CH) ** -0.5),
        "s5_c_re": nrm(ks[17], (L, S5_GROUPS, S5_CH, S5_STATE), S5_STATE ** -0.5),
        "s5_c_im": nrm(ks[18], (L, S5_GROUPS, S5_CH, S5_STATE), S5_STATE ** -0.5),
        "s5_d": nrm(ks[19], (L, S5_GROUPS, S5_CH), 1.0),
        "s5_glu_w": nrm(ks[20], (L, S5_WIDTH, S5_WIDTH), S5_WIDTH ** -0.5),
        "s5_glu_b": nrm(ks[21], (L, S5_WIDTH), 0.01),
        "w_out": nrm(ks[22], (L, D_MIX, D), D_MIX ** -0.5),
        "router_w": nrm(ks[23], (L, D, N_EXPERTS), D ** -0.5),
        "router_b": nrm(ks[24], (L, N_EXPERTS), 0.01),
        "exp_w_gu": nrm(ks[25], (L, N_EXPERTS, D, 2 * D_FF_2), D ** -0.5),
        "exp_b_gu": nrm(ks[26], (L, N_EXPERTS, 2 * D_FF_2), 0.01),
        "exp_w_down": nrm(ks[27], (L, N_EXPERTS, D_FF_2, D), D_FF_2 ** -0.5),
        "exp_b_down": nrm(ks[28], (L, N_EXPERTS, D), 0.01),
    }

def second_block(x, c, ada_w, ada_b, mix_pre_g, mix_post_g, ffn_pre_g, ffn_post_g, w_in, w_alpha, b_alpha,
              gla_norm_g, s5_lambda_re, s5_lambda_im, s5_log_dt, s5_b_re, s5_b_im, s5_c_re, s5_c_im, s5_d,
              s5_glu_w, s5_glu_b, w_out, router_w, router_b, exp_w_gu, exp_b_gu, exp_w_down, exp_b_down):
    B_, T_, D_ = x.shape
    h = x
    for l in range(DEPTH_2):
        mod = jax.nn.silu(c) @ ada_w[l] + ada_b[l]
        sh1, sc1, g1, sh2, sc2, g2 = jnp.split(mod, 6, axis=-1)

        hn = rmsnorm(h, mix_pre_g[l]) * (1.0 + sc1[:, None, :]) + sh1[:, None, :]
        proj = hn @ w_in[l]
        q, k, v, og, a_lr, u = jnp.split(proj, SPLITS, axis=-1)

        def heads(t, dh):
            return t.reshape(B_, T_, GLA_HEADS, dh).transpose(0, 2, 1, 3)

        log_a = jax.nn.log_sigmoid((a_lr @ w_alpha[l] + b_alpha[l]).astype(jnp.float32)) / GLA_TAU
        o = gla_chunked(heads(q, GLA_DK), heads(k, GLA_DK), heads(v, GLA_DV), heads(log_a, GLA_DK))
        o = rmsnorm(o, gla_norm_g[l]).transpose(0, 2, 1, 3)
        gla_out = (o * jax.nn.silu(og.astype(jnp.float32)).reshape(B_, T_, GLA_HEADS, GLA_DV))
        gla_out = gla_out.reshape(B_, T_, GLA_WIDTH).astype(hn.dtype)

        s5_out = s5_layer(u, s5_lambda_re[l], s5_lambda_im[l], s5_log_dt[l], s5_b_re[l], s5_b_im[l],
                          s5_c_re[l], s5_c_im[l], s5_d[l], s5_glu_w[l], s5_glu_b[l]).astype(hn.dtype)

        mix = jnp.concatenate([gla_out, s5_out], axis=-1) @ w_out[l]
        h = h + g1[:, None, :] * rmsnorm(mix, mix_post_g[l])

        hn2 = rmsnorm(h, ffn_pre_g[l]) * (1.0 + sc2[:, None, :]) + sh2[:, None, :]
        ff = moe_ffn(hn2, router_w[l], router_b[l], exp_w_gu[l], exp_b_gu[l], exp_w_down[l], exp_b_down[l])
        h = h + g2[:, None, :] * rmsnorm(ff, ffn_post_g[l])
    return h


def setup_inputs(seed=0):
    out = dict(first_inputs(seed))
    for name, value in second_inputs(seed + 1).items():
        if name != "x":
            out[name + "_2"] = value
    return out


def reference(
    x, attn_norm, w_in, w_out, nsa_q_gain, nsa_k_gain, cmp_pe, cmp_w1, cmp_w2, gm_ws, gm_b,
    ffn_norm, w_gate_up, w_down, rel_bias, c_2, ada_w_2, ada_b_2, mix_pre_g_2, mix_post_g_2,
    ffn_pre_g_2, ffn_post_g_2, w_in_2, w_alpha_2, b_alpha_2, gla_norm_g_2, s5_lambda_re_2,
    s5_lambda_im_2, s5_log_dt_2, s5_b_re_2, s5_b_im_2, s5_c_re_2, s5_c_im_2, s5_d_2, s5_glu_w_2,
    s5_glu_b_2, w_out_2, router_w_2, router_b_2, exp_w_gu_2, exp_b_gu_2, exp_w_down_2,
    exp_b_down_2,
):
    x = first_block(
        x, attn_norm, w_in, w_out, nsa_q_gain, nsa_k_gain, cmp_pe, cmp_w1, cmp_w2, gm_ws, gm_b,
        ffn_norm, w_gate_up, w_down, rel_bias,
    )
    return second_block(
        x, c_2, ada_w_2, ada_b_2, mix_pre_g_2, mix_post_g_2, ffn_pre_g_2, ffn_post_g_2, w_in_2,
        w_alpha_2, b_alpha_2, gla_norm_g_2, s5_lambda_re_2, s5_lambda_im_2, s5_log_dt_2,
        s5_b_re_2, s5_b_im_2, s5_c_re_2, s5_c_im_2, s5_d_2, s5_glu_w_2, s5_glu_b_2, w_out_2,
        router_w_2, router_b_2, exp_w_gu_2, exp_b_gu_2, exp_w_down_2, exp_b_down_2,
    )


_drawn_inputs = setup_inputs


def setup_inputs(seed=0):
    import zlib

    import numpy as np

    out = dict(_drawn_inputs(seed))
    spreads = {}
    factors = {'nsa_q_gain': 8.0,
     'nsa_k_gain': 8.0,
     'gm_b': 3.543,
     'mix_post_g_2': 3.163,
     'ffn_post_g_2': 4.708,
     'b_alpha_2': 2.954,
     'gla_norm_g_2': 3.2,
     's5_lambda_re_2': 200.0,
     's5_lambda_im_2': 2.74,
     's5_log_dt_2': 2.872,
     's5_b_re_2': 13.504,
     's5_b_im_2': 10.036,
     's5_c_re_2': 3.508,
     's5_c_im_2': 3.536,
     's5_glu_b_2': 8.0,
     'router_b_2': 4.303,
     'exp_b_gu_2': 8.0,
     'exp_b_down_2': 8.0}
    for name, (base, spread) in spreads.items():
        noise = np.random.default_rng([zlib.crc32(name.encode()), seed]).standard_normal(out[name].shape)
        drawn = base * np.exp(spread * noise) if base else spread * noise
        out[name] = __import__('jax').numpy.asarray(drawn.astype(out[name].dtype))
    for name, factor in factors.items():
        out[name] = (out[name] * factor).astype(out[name].dtype)
    return out
```

```python
from contextlib import ExitStack

import numpy as np

import concourse.bass as bass
from concourse import mybir

F32 = mybir.dt.float32
I32 = mybir.dt.int32
U32 = mybir.dt.uint32
ALU = mybir.AluOpType
ACT = mybir.ActivationFunctionType
AX_X = mybir.AxisListType.X

P = 128
T, TT = 256, 2
D, KC = 1024, 8
DEPTH = 2
EPS = 1e-6
NEG = -1e30
GELU_A, GELU_B = 0.7978845608028654, 0.044715

HD, NH = 64, 6
RQ, RV, RG = 0, 2 * NH * HD, 3 * NH * HD
NQ, NKV = 4 * NH * HD, 5 * NH * HD
NG = NKV + 3 * 2 * 2 * HD
GM = NG + 3 * NH
IN_W = GM + 512
WIN_BLOCKS = -(-IN_W // 512)
WIN_LAST = IN_W - 512 * (WIN_BLOCKS - 1)
FF = 2816
FF_BLOCKS, FF_TILES = FF // 256, FF // 128
NCMP = 15
WIN_BUCKETS = 32

PC_ATTN, PC_FFN, PC_QG, PC_KG, PC_GB, PC_PE, PC_WS, PC_W2 = 0, 8, 16, 17, 20, 24, 56, 568
PC_N = 568 + 128

K_ID, K_FLIP, K_COS, K_SIN, K_DEC, K_TRI = 0, 128, 256, 320, 384, 384 + 6 * 256
K_CM = K_TRI + 128
K_SUT, K_ONE, K_IOTA, K_E32, K_RST, K_SEL, K_GM = (K_CM + 32 + i for i in (0, 128, 256, 384, 416, 672, 800))
K_ALL = K_GM + 128

N_EXPERTS = 32
SWIGLU_ALPHA, SWIGLU_LIMIT = 1.702, 7.0
TWO_PI = 6.283185307179586
TWO_PI_HI = 6.28125
ROUND = 1.5 * 2 ** 23
Q_MPRE, Q_FPRE, Q_ADB, Q_BAL, Q_LRE, Q_LIM, Q_LDT, Q_D, Q_GLB, Q_WA, Q_WL, Q_RW, Q_C, Q_RB, Q_BD = (
    0, 8, 16, 64, 66, 82, 98, 114, 118, 122, 378, 506, 762, 770, 802)
Q_N = 802 + 1024
DT, MAG, ANG, SIN_, COS_, T1, T2, ABR, ABI, FRE, FIM, GLB = (slice(16 * i, 16 * i + 16) for i in range(12))
ACT_STEPS, DVE_STEPS, MOE_STEPS = 21, 246, 9


def shape_constants():
    k = np.zeros((P, K_ALL), np.float32)
    p = np.arange(P)
    k[:, K_ID:K_ID + P] = np.eye(P)
    k[:, K_FLIP:K_FLIP + P] = np.eye(P)[::-1]
    inv = np.float32(10000.0) ** (-np.arange(32, dtype=np.float32) / np.float32(32))
    pos = (np.arange(TT)[None, :] * P + p[:, None]).astype(np.float32)
    ang = pos[:, :, None] * inv[None, None, :]
    k[:, K_COS:K_COS + 64] = np.cos(ang).reshape(P, 64)
    k[:, K_SIN:K_SIN + 64] = np.sin(ang).reshape(P, 64)
    t = np.arange(T)
    for h in range(NH):
        lg = np.log(1.0 - 2.0 ** (-5.0 - h))
        d = t[None, :] - p[:, None]
        k[:, K_DEC + h * T:K_DEC + (h + 1) * T] = np.where(d >= 0, np.exp(np.maximum(d, 0) * lg), 0.0) * HD ** -0.5
    k[:, K_TRI:K_TRI + P] = p[None, :] >= p[:, None]
    end = 16 * np.arange(NCMP) + 31
    k[:, K_CM:K_CM + 30] = ((np.arange(TT)[None, :, None] * P + p[:, None, None]) >= end).reshape(P, 30)
    k[:, K_SUT:K_SUT + P] = p[:, None] < p[None, :]
    k[:, K_ONE:K_ONE + P] = 1.0
    k[:, K_IOTA:K_IOTA + P] = p % 64
    k[:, K_E32:K_E32 + 32] = np.arange(32)
    k[:, K_RST:K_RST + T] = t % 64 != 0
    k[:, K_SEL:K_SEL + P] = (p % 32 == 0)[:, None]
    k[:, K_GM:K_GM + P] = (p[:, None] <= p[None, :]) & (p[:, None] // 64 == p[None, :] // 64)
    return k


def bucket_constants():
    k = np.zeros((WIN_BUCKETS, 1024), np.float32)
    dist = 255 - np.arange(511)
    n = np.maximum(dist, 0)
    nf = np.maximum(n, 1).astype(np.float32)
    large = 16 + (np.log(nf / np.float32(16)) / np.float32(np.log(8.0)) * np.float32(16)).astype(np.int32)
    bucket = np.where(n < 16, n, np.minimum(large, 31))
    k[bucket, np.arange(511)] = 1.0
    k[0:NH, 512:1023] = np.where(dist < 0, NEG, 0.0)[None, :]
    return k


class Link:

    def __init__(self, eng, sem):
        self.eng, self.sem, self.base, self.n = eng, sem, 0, 0

    def __call__(self, ins):
        self.n += 1
        ins.then_inc(self.sem, 1)
        self.eng.wait_ge(self.sem, self.base + self.n)

    def to(self, ins, sem, value):
        ins.then_inc(sem, 1)
        self.eng.wait_ge(sem, value)

    def enter(self, i, steps):
        self.start, self.steps = self.base + self.n, steps
        self.base, self.n = i * steps + self.start, 0

    def leave(self, trips):
        assert self.n == self.steps, ("links in the loop", self.n, self.steps)
        self.base, self.n = self.start + trips * self.steps, 0


def stream_plan():
    layer = [("win", n) for n in range(WIN_BLOCKS)] + [("cw1", 0)] + [("wout", n) for n in range(2)]
    for i in range(FF_BLOCKS):
        layer.append(("gu", i))
        if i % 2 == 1 or i == FF_BLOCKS - 1:
            layer.append(("dn", i // 2))
    return layer


RING = 6
LAYER_LOADS = stream_plan()
PLACE = {key: (n % RING, n // RING) for n, key in enumerate(LAYER_LOADS)}
SLOT_USES = [sum(1 for n in range(len(LAYER_LOADS)) if n % RING == s) for s in range(RING)]


def second_plan():
    keys = [("ada", n) for n in range(12)] + [("win2", n) for n in range(4)] + [("glu", 0), ("wout2", 0), ("wout2", 1)]
    slots = [3, 4, 5, 0, 1, 2, 0, 1, 2, 0, 1, 2, 0, 1, 2, 0, 1, 2, 0]
    done = [DEPTH * u for u in SLOT_USES]
    place = {}
    for key, slot in zip(keys, slots):
        place[key] = (slot, done[slot], done[slot])
        done[slot] += 1
    return keys, place, done, [n + (s >= 3) for s, n in enumerate(done)]


LOADS_2, PLACE_2, LOADS_BEFORE, USES_BEFORE = second_plan()


def combos():
    return [(br, h) for br in range(2) for h in range(NH)]


def counts_before(steps):
    at, out = 0, {}
    for name, n in steps:
        out[name] = at
        at += n
    return out


PE2 = counts_before([("r_xt", 1), ("r_u", 1), ("r_qk0", 1), ("r_qk", 1), ("r_vo", 4), ("r_al", 1), ("r_ket", 1), ("r_sc", 1),
    ("r_dl", 1), ("r_o", 1), ("r_ot", 1), ("u_glu", 1), ("r_wo", 1), ("r_xt3", 1), ("r_xb", 1), ("m_lg", 1), ("m_rk", 1), ("m_bd",
    1)])
DVE2 = counts_before([("r_cs", 1), ("r_xn", 1), ("u_ang", 1), ("u_cs", 1), ("u_cm", 1), ("r_mc", 1), ("r_hd", 1), ("r_ue", 1),
    ("r_qke", 1), ("r_z", 1), ("r_b", 1), ("r_qd", 1), ("r_scd", 1), ("r_st", 1), ("r_go", 1), ("u_g1", 1), ("u_yg", 1), ("u_out",
    1), ("r_xn3", 1), ("r_hd3", 1), ("r_xbd", 1), ("m_top", 1), ("m_ch", 1), ("m_rounds", 1), ("m_go", 1), ("r_done", 1)])
ACT2 = counts_before([("r_c", 1), ("u_dt", 1), ("u_sin", 1), ("r_ade", 12), ("r_ha", 1), ("r_voe", 4), ("r_ln", 1), ("r_e", 1),
    ("r_sg", 1), ("r_kee", 1), ("r_osq", 1), ("r_ote", 1), ("u_g2", 1), ("u_sg", 1), ("r_ss", 1), ("r_ha3", 1), ("r_xbe", 1),
    ("m_exp", 1)])


def program(nc, a, out, scratch):
    ctx = ExitStack()
    with ctx:
        def sb(name, shape, dt=F32):
            return ctx.enter_context(nc.sbuf_tensor(name, shape, dt))

        def sem(name):
            return ctx.enter_context(nc.semaphore(name))

        ring = sb("ring", [P, RING, 4096])
        x = sb("x", [P, TT, D])
        xn = sb("xn", [P, TT, D])
        hT = sb("hT", [P, KC, T])
        proj = sb("proj", [P, TT, IN_W])
        tb = sb("tb", [P, TT, 11, P])
        tT = sb("tT", [P, 13, T])
        blocks = sb("blocks", [P, 2, 2, NCMP * 16])
        par = sb("par", [P, PC_N])
        bm = sb("bm", [P, NH, T])
        K = sb("K", [P, K_ALL])
        tmp = sb("tmp", [P, 1536])
        st = sb("st", [P, 256])
        sti = sb("sti", [P, 32], I32)
        hid = sb("hid", [64, 4, 60])
        kc = sb("kc", [32, 4, P])
        vc = sb("vc", [NCMP, P])
        kcT = sb("kcT", [P, 32])
        pcm = sb("pcm", [P, TT, NH, NCMP])
        PS = ctx.enter_context(nc.psum_tensor("PS", [P, 8, 512], F32))

        mix = xn
        hTf = hT[:, :, :].rearrange("p k t -> p (k t)")
        S = [hTf[:, 384 * i:384 * (i + 1)] for i in range(3)]
        PT = [hTf[:, 1152 + 384 * i:1152 + 384 * (i + 1)] for i in range(2)]
        tbf = tb[:, :, :, :].rearrange("p a b c -> p (a b c)")
        pcT = tbf[0:NCMP, 0:12 * P].rearrange("p (c t) -> p c t", c=12)
        ident = K[:, K_ID:K_ID + P]
        act_T = [tT[:, 2 * i:2 * i + 2, :].rearrange("p a t -> p (a t)") for i in range(2)]
        th_T = [tT[:, 4 + 2 * i:6 + 2 * i, :].rearrange("p a t -> p (a t)") for i in range(2)]

        pf = proj[:, :, :].rearrange("p t c -> p (t c)")
        p2 = pf[:, 0:Q_N]
        g_row = pf[:, Q_N:Q_N + 2048]
        post = pf[:, Q_N + 2048:Q_N + 4096]
        ssm = tbf[:, 0:2048].rearrange("p (i n) -> p i n", i=4)
        cneg = tbf[:, 2048:2560]
        gla_g = tbf[:, 2560:2688]
        tTf = tT[:, :, :].rearrange("p a t -> p (a t)")
        uT = tTf[:, 0:1024].rearrange("p (q t) -> p q t", q=4)
        yT = uT
        qk2 = tTf[:, 1024:2048].rearrange("p (q t) -> p q t", q=4)
        yw = tTf[:, 1024:2048]
        la, lb = tTf[:, 2048:2560], tTf[:, 2560:3072]
        alr = tTf[0:16, 3072:3328]
        bmf = bm[:, :, :].rearrange("p h t -> p (h t)")
        eb, ee = bmf[:, 0:512], bmf[:, 512:1024]
        ke = bmf[:, 1024:1536].rearrange("p (t c) -> p t c", t=TT)
        modr = [tmp[:, 0:512], tmp[:, 512:1024]]
        vv2 = tmp[:, 0:1024].rearrange("p (t c) -> p t c", t=TT)
        blf = blocks[:, :, :, :].rearrange("p a b c -> p (a b c)")
        cs, mc, s5v, ph = blf[:, 0:264], blf[:, 264:296], blf[:, 300:492], blf[:, 500:516]
        paux = par[:, 0:512]
        og, sgate = xn[:, :, 0:512], xn[:, :, 512:1024]
        sct = hTf[:, 0:1024].rearrange("p (c t) -> p c t", c=8)
        osq = hTf[:, 1024:2048]
        etab = ring[:, 3, :].rearrange("p (b i n) -> p b i n", b=2, i=2)
        etab3 = [etab[:, 0], etab[:, 1], post.rearrange("p (i n) -> p i n", i=2)]
        zy = ring[:, 4, :].rearrange("p (i n) -> p i n", i=4)
        pp = ring[:, 5, :].rearrange("p (i n) -> p i n", i=4)
        gst = ring[:, 5, 0:768].rearrange("p (c n) -> p c n", c=3)
        bgu = tTf[0:32, 0:2048]
        mgs, mth = tTf[:, 2048:2560], tTf[:, 2560:3072]
        gT = tTf[0:32, 3072:3328]
        mus, aT, ysb, xg = (tbf[:, 512 * i:512 * i + 512] for i in range(4))
        hot1, hotw = (tbf[:, 2048 + 256 * i:2304 + 256 * i].rearrange("p (t m) -> p t m", t=TT) for i in range(2))
        pwT = tbf[:, 2560:2816]
        mst = bmf[:, 0:128]
        gates, chosen, rank = (bmf[:, 128 + 64 * i:192 + 64 * i].rearrange("p (t e) -> p t e", t=TT) for i in range(3))
        oh2, esel = bmf[:, 320:352], bmf[0:32, 352:416]
        mix_i = bmf[:, 416:432].bitcast(U32)
        item_i = bmf[:, 432:496].bitcast(I32)
        oacc = hTf.rearrange("p (t n) -> p t n", t=TT)
        tmp2 = tmp[:, 0:1024]

        names = """s_dve s_act s_pe s_pool s_x s_k s_oh s_par s_xn s_xt s_hd s_ha s_pj s_pd s_pa s_rope s_nk s_t0 s_t1 s_t2 s_e1 s_e2 s_e3
            s_g1 s_g2 s_g3 s_gp s_c1 s_c2 s_c3 s_c4 s_c5 s_c6 s_c7 s_c8 s_c9 s_c10 s_c11 s_c12 s_c13 s_c14 s_c15 s_rs s_rd s_rp
            s_rp2 s_rq s_rm s_rg s_gt s_cm s_sc s_sd s_ex s_tp s_pe2 s_pv s_mix s_mt s_md s_ma s_wo s_xn2 s_xt2 s_hd2 s_ha2 s_gu
            s_th s_actv s_dn s_b0 s_b1 s_b2 s_b3 s_b4 s_out s_ld r_par r_ssm r_row r_ada r_adc u_e u_bu u_bd u_pd u_c u_pl m_bg m_p
            m_xg m_xge m_pw m_pwe m_gu m_gs m_th m_a m_at m_ate m_y m_ye m_s m_sd m_es m_dve m_f pe2 dve2 act2""".split()
        sems = {n: sem(n) for n in names}
        g = type("Semaphores", (), sems)
        landed = [sem(f"landed{i}") for i in range(RING)]
        freed = [sem(f"freed{i}") for i in range(RING)]

        block = ctx.enter_context(nc.Block())

        def source(key, l):
            kind, n = key
            if kind == "cw1":
                return a["cmp_w1"][l], 2048
            if kind == "win":
                if n == WIN_BLOCKS - 1:
                    return a["w_in_last"][l], KC * WIN_LAST
                return a["w_in_blocks"][l, n], 4096
            if kind == "wout":
                return a["w_out"][l, n], 4096
            if kind == "gu":
                return a["w_gate_up"][l, n], 4096
            m = min(4, FF_TILES - 4 * n)
            return a["w_down"][l, :, 4 * n * D:(4 * n + m) * D], m * D

        def source_2(key):
            kind, n = key
            if kind == "glu":
                return a["s5_glu_w"], 2048
            return {"ada": a["ada_w"], "win2": a["w_in_2"], "wout2": a["w_out_2"]}[kind][n], 4096

        @block.sync
        def _(sp):
            sp.dma_start(x[:], a["x"][0].rearrange("(t p) d -> p t d", p=P)).then_inc(g.s_x, 16)
            sp.dma_start(K[:], a["constants"]).then_inc(g.s_k, 16)
            sp.dma_start(tb[0:WIN_BUCKETS, 0, 0:9, :].rearrange("p a b -> p (a b)")[:, 0:1024], a["buckets"]).then_inc(g.s_oh, 16)
            sp.dma_start(kc[0:WIN_BUCKETS, 0, 0:NH], a["rel_bias"]).then_inc(g.s_oh, 16)
            sp.wait_ge(g.s_par, 16)
            with sp.Fori(0, DEPTH) as l:
                for n, key in enumerate(LAYER_LOADS):
                    slot, use = PLACE[key]
                    sp.wait_ge(freed[slot], l * SLOT_USES[slot] + use + 1)
                    src, width = source(key, l)
                    sp.dma_start(ring[:, slot, 0:width], src).then_inc(landed[slot], 16)
            def load_2(key):
                slot, load, use = PLACE_2[key]
                sp.wait_ge(freed[slot], use + 1)
                src, width = source_2(key)
                sp.dma_start(ring[:, slot, 0:width], src).then_inc(landed[slot], 16)

            for key in LOADS_2[0:3]:
                load_2(key)
            sp.wait_ge(g.s_ld, DEPTH + 2)
            sp.dma_start(p2, a["params_2"]).then_inc(g.r_par, 16)
            sp.dma_start(ssm.rearrange("p i n -> p (i n)"), a["ssm_matrices"]).then_inc(g.r_ssm, 16)
            sp.dma_start(g_row, a["ada_b_gates"].broadcast_to([P, 2048])).then_inc(g.r_row, 16)
            sp.dma_start(post, a["post_gains"].broadcast_to([P, 2048])).then_inc(g.r_row, 16)
            sp.dma_start(gla_g, a["gla_norm_g"].broadcast_to([P, 128])).then_inc(g.r_row, 16)
            for key in LOADS_2[3:]:
                load_2(key)

            def expert(e, n):
                for slot in range(RING):
                    sp.wait_ge(freed[slot], n + USES_BEFORE[slot] + 1)
                    if slot < 4:
                        src = a["exp_w_gu"][e, 2 * slot * P:(2 * slot + 2) * P, :].rearrange("(c p) n -> p c n", p=P)
                        dst = ring[:, slot, :].rearrange("p (c n) -> p c n", c=2)
                    else:
                        src = a["exp_w_down"][e, 4 * (slot - 4) * P:(4 * (slot - 4) + 4) * P, :].rearrange("(c p) n -> p c n", p=P)
                        dst = ring[:, slot, :].rearrange("p (c n) -> p c n", c=4)
                    sp.dma_start(dst, src).then_inc(landed[slot], 16)

            with sp.Fori(0, N_EXPERTS) as e:
                expert(e, e)
            sp.wait_ge(g.dve2, DVE2["m_rounds"] + 1)
            items = sp.value_load(item_i[0:1, 63:64], min_val=N_EXPERTS, max_val=N_EXPERTS + 16)
            with sp.If(items > N_EXPERTS):
                with sp.Fori(N_EXPERTS, items) as n:
                    expert(sp.value_load(item_i[0:1, bass.ds(n, 1)], min_val=0, max_val=N_EXPERTS - 1), n)
            sp.wait_ge(g.dve2, DVE2["r_done"] + 1)
            sp.dma_start(out[0].rearrange("(t p) d -> p t d", p=P), x[:]).then_inc(g.s_out, 16)
            sp.wait_ge(g.s_out, 16)

        @block.scalar
        def _(act):
            link = Link(act, g.s_act)

            def evac_transposed(done, first, gain, value):
                for b in (1, 3):
                    for k in (0, 1):
                        c = 2 * b + k
                        src = PS[:, first + b, 256 * k:256 * k + 256]
                        if gain is None:
                            ins = nc.scalar.activation(hT[:, c, :], src, ACT.Copy)
                        else:
                            ins = nc.scalar.activation(hT[:, c, :], src, ACT.Copy, scale=par[:, gain + c:gain + c + 1])
                        if c == 7:
                            link.to(ins, done, value)
                        else:
                            link(ins)

            act.wait_ge(g.s_b0, 1)
            act.dma_start(scratch, tmp[0:NH, 0:512]).then_inc(g.s_b1, 16)
            act.wait_ge(g.s_b1, 16)
            src = bass.AP(scratch.tensor, 0, [[1, P], [512, NH], [1, T]])
            act.dma_start(proj[:, 0, 0:NH * T].rearrange("p (h t) -> p h t", h=NH), src).then_inc(g.s_b2, 16)
            with act.Fori(0, DEPTH) as l:
                link.enter(l, ACT_STEPS)
                act.wait_ge(g.s_ld, l + 1)
                act.dma_start(par[:], a["layer_params"][l]).then_inc(g.s_par, 16)
                act.wait_ge(g.s_par, 16 * l + 16)
                act.wait_ge(g.s_xt, l + 1)
                evac_transposed(g.s_ha, 4, PC_ATTN, l + 1)
                for nb in range(WIN_BLOCKS):
                    w = 512 if nb < WIN_BLOCKS - 1 else WIN_LAST
                    act.wait_ge(g.s_pj, l * 14 + 2 * nb + 2)
                    link.to(nc.scalar.activation(proj[:, 1, 512 * nb:512 * nb + w], PS[:, (2 * nb + 1) % 8, 0:w], ACT.Copy),
                            g.s_pa, l * 7 + nb + 1)
                act.wait_ge(g.s_pd, l * 7 + 7)
                link.to(nc.scalar.activation(mix[:, :, 0:384], proj[:, :, RG:RG + 384], ACT.Tanh, scale=0.5), g.s_rg, l + 1)
                link.to(nc.scalar.activation(st[:, 0:36].rearrange("p (t c) -> p t c", t=TT), proj[:, :, NG:NG + 18], ACT.Tanh, scale=0.5),
                        g.s_gt, l + 1)
                act.wait_ge(g.s_t1, l + 1)
                link.to(nc.scalar.activation(tT[:, 0:6, :].rearrange("p (b c) t -> p b (c t)", b=3), PS[:, 0:3, :], ACT.Copy), g.s_e1, l + 1)
                act.wait_ge(g.s_g1, l + 1)
                link.to(nc.scalar.activation(tmp[:, 0:1024], tmp[:, 0:1024], ACT.Tanh, scale=GELU_A), g.s_g2, l + 1)
                act.wait_ge(g.s_c2, l + 1)
                link.to(nc.scalar.activation(hid[:, 1, :], hid[:, 1, :], ACT.Tanh, scale=GELU_A), g.s_c3, l + 1)
                act.wait_ge(g.s_rp, l + 1)
                act.wait_ge(g.s_g3, l + 1)
                link.to(nc.scalar.activation(tmp[:, 0:768].rearrange("p (t c) -> p t c", t=TT), PS[:, 3:5, 0:384], ACT.Square), g.s_rq, l + 1)
                act.wait_ge(g.s_c10, l + 1)
                link.to(nc.scalar.activation(pcm[:], pcm[:], ACT.Exp), g.s_c11, l + 1)
                act.wait_ge(g.s_c13, l + 1)
                link.to(nc.scalar.activation(pcT, PS[0:NCMP, 0:3, :].rearrange("p b (c t) -> p (b c) t", c=4), ACT.Copy), g.s_c14, l + 1)
                for i in range(13):
                    if i < 12:
                        act.wait_ge(g.s_sd, l * 12 + i + 1)
                        link(nc.scalar.activation(S[i % 3][:, 0:256], S[i % 3][:, 0:256], ACT.Exp, bias=st[:, 64 + 2 * i + 1:64 + 2 * i + 2],
                                                  accum_out=st[:, 96 + 2 * i + 1:96 + 2 * i + 2]))
                        link.to(nc.scalar.activation(S[i % 3][:, 256:384], S[i % 3][:, 256:384], ACT.Exp, bias=st[:, 64 + 2 * i:64 + 2 * i + 1],
                                                     accum_out=st[:, 96 + 2 * i:96 + 2 * i + 1]), g.s_ex, l * 12 + i + 1)
                    if i >= 1:
                        c = i - 1
                        act.wait_ge(g.s_tp, l * 12 + c + 1)
                        if c >= 2:
                            act.wait_ge(g.s_pv, l * 12 + c - 1)
                        link.to(nc.scalar.activation(PT[c % 2], PS[:, 3 + c % 2, 0:384], ACT.Copy), g.s_pe2, l * 12 + c + 1)
                act.wait_ge(g.s_mt, l + 1)
                act.wait_ge(g.s_pv, l * 12 + 12)
                evac_transposed(g.s_ma, 0, None, l + 1)
                act.wait_ge(g.s_xt2, l + 1)
                evac_transposed(g.s_ha2, 0, PC_FFN, l + 1)
                for i in range(FF_BLOCKS):
                    act.wait_ge(g.s_gu, l * FF_BLOCKS + i + 1)
                    if i >= 2:
                        act.wait_ge(g.s_actv, l * FF_BLOCKS + i - 1)
                    link.to(nc.scalar.activation(th_T[i % 2], PS[:, 4 + 2 * (i % 2), :], ACT.Tanh, scale=0.5), g.s_th, l * FF_BLOCKS + i + 1)
            link.leave(DEPTH)
            act.wait_ge(g.r_par, 16)
            link.to(nc.scalar.activation(cs[:, 0:8], p2[:, Q_C:Q_C + 8], ACT.Tanh, scale=0.5), g.act2, ACT2["r_c"] + 1)
            link.to(nc.scalar.activation(s5v[:, DT], p2[:, Q_LDT:Q_LDT + 16], ACT.Exp), g.act2, ACT2["u_dt"] + 1)
            act.wait_ge(g.dve2, DVE2["u_ang"] + 1)
            link(nc.scalar.activation(s5v[:, MAG], s5v[:, MAG], ACT.Exp))
            link(nc.scalar.activation(s5v[:, SIN_], s5v[:, ANG], ACT.Sin))
            link.to(nc.scalar.activation(s5v[:, COS_], s5v[:, ANG], ACT.Sin, scale=0.5), g.act2, ACT2["u_sin"] + 1)
            for n in range(12):
                act.wait_ge(g.r_ada, n + 1)
                if n >= 2:
                    act.wait_ge(g.r_adc, n - 1)
                link.to(nc.scalar.activation(modr[n % 2], PS[:, n % 2, :], ACT.Copy), g.act2, ACT2["r_ade"] + n + 1)

            def evac_2(first, done, value, col):
                for b in (1, 3):
                    for k in (0, 1):
                        c = 2 * b + k
                        ins = nc.scalar.activation(hT[:, c, :], PS[:, first + b, 256 * k:256 * k + 256], ACT.Identity,
                                                   bias=mc[:, col + c:col + c + 1], scale=mc[:, col + 8 + c:col + 9 + c])
                        if c == 7:
                            link.to(ins, done, value)
                        else:
                            link(ins)

            act.wait_ge(g.dve2, DVE2["r_mc"] + 1)
            act.wait_ge(g.pe2, PE2["r_xt"] + 1)
            evac_2(4, g.act2, ACT2["r_ha"] + 1, 0)
            for n in range(4):
                act.wait_ge(g.pe2, PE2["r_vo"] + n + 1)
                b, t = n // 2, n % 2
                link.to(nc.scalar.activation((vv2 if b == 0 else og)[:, t, :], PS[:, 4 + n, :], ACT.Copy), g.act2, ACT2["r_voe"] + n + 1)
            act.wait_ge(g.dve2, DVE2["r_z"] + 1)
            link(nc.scalar.activation(lb, lb, ACT.Exp, scale=-1.0))
            link.to(nc.scalar.activation(lb, lb, ACT.Ln, bias=K[:, K_ONE:K_ONE + 1]), g.act2, ACT2["r_ln"] + 1)
            act.wait_ge(g.dve2, DVE2["r_b"] + 1)
            link(nc.scalar.activation(eb, la, ACT.Exp))
            link(nc.scalar.activation(lb, la, ACT.Exp, scale=-1.0))
            for p in range(2):
                for c in range(4):
                    o = 256 * p + 64 * c
                    ins = nc.scalar.activation(ee[:, o:o + 64], la[:, o:o + 64], ACT.Exp, scale=-1.0, bias=la[:, o + 63:o + 64])
                    if p == 1 and c == 3:
                        link.to(ins, g.act2, ACT2["r_e"] + 1)
                    else:
                        link(ins)
            link.to(nc.scalar.activation(sgate, og, ACT.Tanh, scale=0.5), g.act2, ACT2["r_sg"] + 1)
            act.wait_ge(g.pe2, PE2["r_ket"] + 1)
            link.to(nc.scalar.activation(ke.rearrange("p t c -> p (t c)"), PS[:, 2, :], ACT.Copy), g.act2, ACT2["r_kee"] + 1)
            act.wait_ge(g.pe2, PE2["r_o"] + 1)
            for b in range(2):
                ins = nc.scalar.activation(osq[:, 512 * b:512 * b + 512], PS[:, 6 + b, :], ACT.Square)
                if b == 0:
                    link(ins)
                else:
                    link.to(ins, g.act2, ACT2["r_osq"] + 1)
            act.wait_ge(g.pe2, PE2["r_ot"] + 1)
            link.to(nc.scalar.activation(hT[:, 0:4, :].rearrange("p (b c) t -> p b (c t)", b=2), PS[:, 6:8, :], ACT.Copy), g.act2, ACT2["r_ote"] + 1)
            act.wait_ge(g.dve2, DVE2["u_g1"] + 1)
            link.to(nc.scalar.activation(yw, yw, ACT.Tanh, scale=GELU_A), g.act2, ACT2["u_g2"] + 1)
            act.wait_ge(g.pe2, PE2["u_glu"] + 1)
            for q in range(4):
                ins = nc.scalar.activation(yw[:, 256 * q:256 * q + 256], PS[:, q // 2, 256 * (q % 2):256 * (q % 2) + 256], ACT.Tanh,
                                           scale=0.5, bias=s5v[:, GLB][:, q:q + 1])
                if q < 3:
                    link(ins)
                else:
                    link.to(ins, g.act2, ACT2["u_sg"] + 1)
            act.wait_ge(g.pe2, PE2["r_wo"] + 1)
            for t in range(TT):
                ins = nc.scalar.activation(tmp[:, 0:1024], PS[:, 2 + 2 * t:4 + 2 * t, :].rearrange("p b n -> p (b n)"), ACT.Square, accum_out=st[:, 230 + t:231 + t])
                if t == 0:
                    link(ins)
                else:
                    link.to(ins, g.act2, ACT2["r_ss"] + 1)
            act.dma_start(bgu, a["exp_b_gu"]).then_inc(g.m_bg, 16)
            act.wait_ge(g.pe2, PE2["r_xt3"] + 1)
            evac_2(4, g.act2, ACT2["r_ha3"] + 1, 16)
            act.wait_ge(g.pe2, PE2["r_xb"] + 1)
            for b in (1, 3):
                ins = nc.scalar.activation(xn[:, b // 2, 512 * (b % 2):512 * (b % 2) + 512], PS[:, b, :], ACT.Copy)
                if b == 1:
                    link(ins)
                else:
                    link.to(ins, g.act2, ACT2["r_xbe"] + 1)
            act.wait_ge(g.dve2, DVE2["m_top"] + 1)
            link.to(nc.scalar.activation(mst[:, 0:8], mst[:, 0:8], ACT.Exp), g.act2, ACT2["m_exp"] + 1)
            act.wait_ge(g.dve2, DVE2["m_rounds"] + 1)
            items = act.value_load(item_i[0:1, 63:64], min_val=N_EXPERTS, max_val=N_EXPERTS + 16)
            act.wait_ge(g.m_xg, 1)
            nc.scalar.activation(xg, PS[:, 3, :], ACT.Copy).then_inc(g.m_xge, 1)
            with act.Fori(0, items) as n:
                act.wait_ge(g.m_gs, n + 1)
                nc.scalar.activation(mth, mgs, ACT.Tanh, scale=0.5 * SWIGLU_ALPHA).then_inc(g.m_th, 1)
                act.wait_ge(g.m_xg, n + 2)
                nc.scalar.activation(xg, PS[:, 3, :], ACT.Copy).then_inc(g.m_xge, 1)
                act.wait_ge(g.m_at, n + 1)
                nc.scalar.activation(aT, PS[:, 4, :], ACT.Copy, scale=0.5).then_inc(g.m_ate, 1)
                act.wait_ge(g.m_y, n + 1)
                nc.scalar.activation(ysb, PS[:, 2, :], ACT.Copy).then_inc(g.m_ye, 1)

        @block.vector
        def _(v):
            link = Link(v, g.s_dve)

            def rsqrt(src, n, parts=P):
                y, q = st[0:parts, 160:160 + n], st[0:parts, 184:184 + n]
                link(v.tensor_scalar(sti[0:parts, 0:n], src.bitcast(I32), 1, None, ALU.logical_shift_right))
                link(v.tensor_scalar(y.bitcast(I32), sti[0:parts, 0:n], -1.0, 1597463007.0, ALU.mult, ALU.add))
                for _ in range(3):
                    link(v.scalar_tensor_tensor(q, y, -0.5, y, ALU.mult, ALU.mult))
                    link(v.tensor_tensor(q, q, src, ALU.mult))
                    link(v.scalar_tensor_tensor(y, q, 1.5, y, ALU.add, ALU.mult))
                return y

            def mean_eps(n, width, parts=P):
                s = st[0:parts, 208:208 + n]
                link(v.tensor_scalar(s, s, 1.0 / width, EPS, ALU.mult, ALU.add))
                return s

            def norm_rows(done, value):
                for t in range(TT):
                    link(v.tensor_tensor_reduce(xn[:, t, :], x[:, t, :], x[:, t, :], 1.0, 0.0, ALU.mult, ALU.add, st[:, 208 + t:209 + t]))
                y = rsqrt(mean_eps(2, D), 2)
                for t in range(TT):
                    ins = v.tensor_scalar(xn[:, t, :], x[:, t, :], y[:, t:t + 1], None, ALU.mult)
                    if t == 0:
                        link(ins)
                    else:
                        link.to(ins, done, value)

            def evac_transposed(done, first, gain, value):
                for b in (0, 2):
                    for k in (0, 1):
                        c = 2 * b + k
                        src = PS[:, first + b, 256 * k:256 * k + 256]
                        if gain is None:
                            ins = v.tensor_copy(hT[:, c, :], src)
                        else:
                            ins = v.tensor_scalar(hT[:, c, :], src, par[:, gain + c:gain + c + 1], None, ALU.mult)
                        if c == 5:
                            link.to(ins, done, value)
                        else:
                            link(ins)

            v.wait_ge(g.s_b3, 1)
            v.wait_ge(g.s_oh, 32)
            oh = tb[0:WIN_BUCKETS, 0, 0:9, :].rearrange("p a b -> p (a b)")
            link.to(v.tensor_tensor(tmp[0:NH, 0:512], PS[0:NH, 0, :], oh[0:NH, 512:1024], ALU.add), g.s_b0, 1)
            v.wait_ge(g.s_b4, 1)
            link(v.tensor_copy(bm[:].rearrange("p (a b) t -> p a (b t)", a=3), PS[:, 1:4, :]))
            v.wait_ge(g.s_x, 16)
            v.wait_ge(g.s_k, 16)
            v.sem_inc(g.s_ld, 1)
            with v.Fori(0, DEPTH) as l:
                link.enter(l, DVE_STEPS)
                norm_rows(g.s_xn, l + 1)
                v.wait_ge(g.s_par, 16 * l + 16)
                v.wait_ge(g.s_xt, l + 1)
                evac_transposed(g.s_hd, 4, PC_ATTN, l + 1)
                for nb in range(WIN_BLOCKS):
                    w = 512 if nb < WIN_BLOCKS - 1 else WIN_LAST
                    v.wait_ge(g.s_pj, l * 14 + 2 * nb + 1)
                    link.to(v.tensor_copy(proj[:, 0, 512 * nb:512 * nb + w], PS[:, (2 * nb) % 8, 0:w]), g.s_pd, l * 7 + nb + 1)
                v.wait_ge(g.s_pa, l * 7 + 7)
                for t in range(TT):
                    src = proj[:, t, 0:768].rearrange("p (h two f) -> p h two f", two=2, f=32)
                    dst = tb[:, t, 0:6, :].rearrange("p a (c two f) -> p (a c) two f", two=2, f=32)
                    cos = K[:, K_COS + 32 * t:K_COS + 32 * t + 32].unsqueeze(1).broadcast_to([P, 12, 32])
                    sin = K[:, K_SIN + 32 * t:K_SIN + 32 * t + 32].unsqueeze(1).broadcast_to([P, 12, 32])
                    aux = tmp[:, 0:384].rearrange("p (h f) -> p h f", h=12)
                    link(v.tensor_tensor(dst[:, :, 0, :], src[:, :, 0, :], cos, ALU.mult))
                    link(v.tensor_tensor(aux, src[:, :, 1, :], sin, ALU.mult))
                    link(v.tensor_tensor(dst[:, :, 0, :], dst[:, :, 0, :], aux, ALU.subtract))
                    link(v.tensor_tensor(dst[:, :, 1, :], src[:, :, 1, :], cos, ALU.mult))
                    link(v.tensor_tensor(aux, src[:, :, 0, :], sin, ALU.mult))
                    ins = v.tensor_tensor(dst[:, :, 1, :], dst[:, :, 1, :], aux, ALU.add)
                    if t == 0:
                        link(ins)
                    else:
                        link.to(ins, g.s_rope, l + 1)
                for t in range(TT):
                    q = proj[:, t, NQ:NQ + 384]
                    kk = proj[:, t, NKV + 256:NKV + 768].rearrange("p (b j c) -> p b j c", b=2, j=2)[:, :, 0, :]
                    sq = tmp[:, 0:640]
                    link(v.tensor_tensor(sq[:, 0:384], q, q, ALU.mult))
                    link(v.tensor_tensor(sq[:, 384:640].rearrange("p (b c) -> p b c", b=2), kk, kk, ALU.mult))
                    link(v.tensor_reduce(st[:, 208:218], sq.rearrange("p (h d) -> p h d", d=HD), AX_X, ALU.add))
                    y = rsqrt(mean_eps(10, HD), 10)
                    link(v.tensor_tensor(tb[:, t, 6:9, :].rearrange("p a (c d) -> p (a c) d", d=HD), q.rearrange("p (h d) -> p h d", d=HD),
                                         y[:, 0:6].unsqueeze(2).broadcast_to([P, 6, HD]), ALU.mult))
                    for b in range(2):
                        ins = v.tensor_tensor(tb[:, t, 9 + b, :].rearrange("p (c d) -> p c d", d=HD), kk[:, b, :].rearrange("p (c d) -> p c d", d=HD),
                                              y[:, 6 + 2 * b:8 + 2 * b].unsqueeze(2).broadcast_to([P, 2, HD]), ALU.mult)
                        if t == 1 and b == 1:
                            link.to(ins, g.s_nk, l + 1)
                        else:
                            link(ins)
                v.wait_ge(g.s_t0, l + 1)
                for j in range(2):
                    for gr in range(2):
                        for h2 in range(2):
                            rows, half = slice(64 * gr, 64 * gr + 64), slice(64 * h2, 64 * h2 + 64)
                            src = PS[rows, 6, 256 * j + 16 * h2:256 * j + 16 * h2 + 240].rearrange("p (i m) -> p i m", m=16)
                            pe = par[half, PC_PE + 16 * j:PC_PE + 16 * j + 16].unsqueeze(1).broadcast_to([64, NCMP, 16])
                            ins = v.tensor_tensor(blocks[half, j, gr, :].rearrange("p (i m) -> p i m", m=16), src, pe, ALU.add)
                            if j + gr + h2 == 3:
                                link.to(ins, g.s_e3, l + 1)
                            else:
                                link(ins)
                z = proj[:, :, GM:GM + 512]
                u = tmp[:, 0:1024].rearrange("p (t c) -> p t c", t=TT)
                link(v.tensor_tensor(u, z, z, ALU.mult))
                link(v.tensor_scalar(u, u, GELU_B, 1.0, ALU.mult, ALU.add))
                link.to(v.tensor_tensor(u, u, z, ALU.mult), g.s_g1, l + 1)
                v.wait_ge(g.s_t2, l + 1)
                qg = par[:, PC_QG:PC_QG + 1]
                link(v.tensor_scalar(tT[:, 6:8, :].rearrange("p a t -> p (a t)"), PS[:, 3, :], qg, HD ** -0.5, ALU.mult, ALU.mult))
                link(v.tensor_scalar(tT[:, 8, :], PS[:, 4, 0:256], qg, HD ** -0.5, ALU.mult, ALU.mult))
                for b in range(2):
                    for gr in range(2):
                        for h2 in range(2):
                            rows = slice(64 * gr, 64 * gr + 64)
                            src = PS[rows, 4, 256:512] if b == 0 else PS[rows, 5, 0:256]
                            ins = v.tensor_scalar(tT[64 * h2:64 * h2 + 64, 9 + 2 * b + gr, :], src, par[rows, PC_KG + 1 + b:PC_KG + 2 + b], None, ALU.mult)
                            if b + gr + h2 == 3:
                                link.to(ins, g.s_e2, l + 1)
                            else:
                                link(ins)
                ws = par[:, PC_WS:PC_WS + 512].rearrange("p (g t) -> p g t", g=4)
                link(v.tensor_tensor(ws, ws, K[:, K_TRI:K_TRI + P].unsqueeze(1).broadcast_to([P, 4, P]), ALU.mult))
                v.wait_ge(g.s_g2, l + 1)
                link(v.tensor_scalar(u, u, 0.5, 0.5, ALU.mult, ALU.add))
                link(v.tensor_tensor(z, z, u, ALU.mult))
                vv = proj[:, :, GM + 256:GM + 512]
                sq = tmp[:, 0:512].rearrange("p (t c) -> p t c", t=TT)
                link(v.tensor_tensor(sq, vv, vv, ALU.mult))
                link(v.tensor_reduce(st[:, 208:216], tmp[:, 0:512].rearrange("p (h d) -> p h d", d=64), AX_X, ALU.add))
                y = rsqrt(mean_eps(8, 64), 8)
                for t in range(TT):
                    vt = vv[:, t, :].rearrange("p (h d) -> p h d", d=64)
                    ins = v.tensor_tensor(vt, vt, y[:, 4 * t:4 * t + 4].unsqueeze(2).broadcast_to([P, 4, 64]), ALU.mult)
                    if t == 0:
                        link(ins)
                    else:
                        link.to(ins, g.s_g3, l + 1)
                v.wait_ge(g.s_c1, l + 1)
                link(v.tensor_copy(hid[:, 0, :], PS[0:64, 7, 0:60]))
                link(v.tensor_tensor(hid[:, 1, :], hid[:, 0, :], hid[:, 0, :], ALU.mult))
                link(v.tensor_scalar(hid[:, 1, :], hid[:, 1, :], GELU_B, 1.0, ALU.mult, ALU.add))
                link.to(v.tensor_tensor(hid[:, 1, :], hid[:, 1, :], hid[:, 0, :], ALU.mult), g.s_c2, l + 1)
                for h in range(NH):
                    v.wait_ge(g.s_rs, l * NH + h + 1)
                    if h >= 3:
                        v.wait_ge(g.s_rp2, l * NH + h - 2)
                    dec = K[:, K_DEC + h * T:K_DEC + (h + 1) * T]
                    link(v.tensor_tensor(S[h % 3][:, 0:256], PS[:, h % 3, 0:256], dec, ALU.mult))
                    link.to(v.tensor_tensor(S[h % 3][:, 256:384], PS[:, h % 3, 256:384], dec[:, 0:128], ALU.mult), g.s_rd, l * NH + h + 1)
                v.wait_ge(g.s_c3, l + 1)
                link(v.tensor_scalar(hid[:, 1, :], hid[:, 1, :], 0.5, 0.5, ALU.mult, ALU.add))
                link.to(v.tensor_tensor(hid[:, 2, :], hid[:, 1, :], hid[:, 0, :], ALU.mult), g.s_c4, l + 1)
                v.wait_ge(g.s_gp, l + 1)
                for gr in range(4):
                    src = PS[:, 5, 128 * gr:128 * gr + 128].rearrange("p (c d) -> p c d", c=TT)
                    link(v.scalar_tensor_tensor(mix[:, :, 768 + 64 * gr:832 + 64 * gr], src, par[:, PC_GB + gr:PC_GB + gr + 1],
                                                proj[:, :, GM + 64 * gr:GM + 64 * gr + 64], ALU.add, ALU.mult))
                v.wait_ge(g.s_c5, l + 1)
                link(v.tensor_copy(kc[0:30, 0, 0:64], PS[0:30, 7, 0:64]))
                link(v.tensor_copy(vc[:], PS[0:NCMP, 7, 64:192]))
                link(v.tensor_tensor(kc[0:30, 1, 0:64], kc[0:30, 0, 0:64], kc[0:30, 0, 0:64], ALU.mult))
                link(v.tensor_reduce(st[0:30, 208:209], kc[0:30, 1, 0:64], AX_X, ALU.add))
                y = rsqrt(mean_eps(1, HD, 30), 1, 30)
                link(v.tensor_scalar(kc[0:30, 2, 0:64], kc[0:30, 0, 0:64], y, None, ALU.mult))
                link.to(v.tensor_scalar(kc[0:30, 2, 64:128], kc[0:30, 0, 0:64], y, None, ALU.mult), g.s_c6, l + 1)
                v.wait_ge(g.s_rq, l + 1)
                v.wait_ge(g.s_rg, l + 1)
                link(v.tensor_reduce(st[:, 208:220], tmp[:, 0:768].rearrange("p (h d) -> p h d", d=HD), AX_X, ALU.add))
                y = rsqrt(mean_eps(12, HD), 12)
                ro = mix[:, :, 0:384]
                link(v.tensor_scalar(ro, ro, 0.5, 0.5, ALU.mult, ALU.add))
                link(v.tensor_tensor(ro, ro, proj[:, :, RG:RG + 384], ALU.mult))
                for t in range(TT):
                    aux = tmp[:, 0:384].rearrange("p (h d) -> p h d", d=HD)
                    link(v.tensor_tensor(aux, PS[:, 3 + t, 0:384].rearrange("p (h d) -> p h d", d=HD),
                                         y[:, 6 * t:6 * t + 6].unsqueeze(2).broadcast_to([P, 6, HD]), ALU.mult))
                    ins = v.tensor_tensor(mix[:, t, 0:384], mix[:, t, 0:384], tmp[:, 0:384], ALU.mult)
                    if t == 0:
                        link(ins)
                    else:
                        link.to(ins, g.s_rm, l + 1)
                v.wait_ge(g.s_c7, l + 1)
                link.to(v.tensor_scalar(kcT[:, 0:30], PS[:, 7, 0:30], par[:, PC_KG:PC_KG + 1], None, ALU.mult), g.s_c8, l + 1)
                link(v.memset(pcm[:, 0, :, :], NEG))
                v.wait_ge(g.s_c9, l + 1)
                for par2 in range(2):
                    src = PS[:, 7 - par2, 0:90].rearrange("p (t h n) -> p t h n", t=TT, h=3)
                    link(v.tensor_tensor(pcm[:, 0, par2::2, 0:7], src[:, 0, :, 0:7], bm[:, par2::2, 159:256:16], ALU.add))
                    link(v.tensor_tensor(pcm[:, 1, par2::2, :], src[:, 1, :, :], bm[:, par2::2, 31:256:16], ALU.add))
                link(v.tensor_reduce(st[:, 36:48], pcm[:].rearrange("p t h n -> p (t h) n"), AX_X, ALU.max))
                pc2 = pcm[:].rearrange("p t h n -> p (t h) n")
                link.to(v.tensor_tensor(pc2, pc2, st[:, 36:48].unsqueeze(2).broadcast_to([P, 12, NCMP]), ALU.subtract), g.s_c10, l + 1)
                v.wait_ge(g.s_c11, l + 1)
                link(v.tensor_reduce(st[:, 48:60], pc2, AX_X, ALU.add))
                for t in range(TT):
                    ins = v.tensor_tensor(pcm[:, t, :, :], pcm[:, t, :, :],
                                          K[:, K_CM + 15 * t:K_CM + 15 * t + 15].unsqueeze(1).broadcast_to([P, 6, NCMP]), ALU.mult)
                    if t == 0:
                        link(ins)
                    else:
                        link.to(ins, g.s_c12, l + 1)
                v.wait_ge(g.s_gt, l + 1)
                gate = st[:, 0:36].rearrange("p (t h b) -> p t h b", t=TT, h=NH)
                link(v.tensor_scalar(st[:, 0:36], st[:, 0:36], 0.5, 0.5, ALU.mult, ALU.add))
                link(v.reciprocal(st[:, 48:60], st[:, 48:60]))
                w12 = st[:, 48:60].rearrange("p (t h) -> p t h", t=TT)
                link(v.tensor_tensor(w12, w12, gate[:, :, :, 0], ALU.mult))
                v.wait_ge(g.s_c15, l + 1)
                for t in range(TT):
                    ins = v.tensor_tensor(mix[:, t, 384:768].rearrange("p (h d) -> p h d", d=HD), PS[:, 6 + t, 0:384].rearrange("p (h d) -> p h d", d=HD),
                                          w12[:, t, :].unsqueeze(2).broadcast_to([P, NH, HD]), ALU.mult)
                    if t == 0:
                        link(ins)
                    else:
                        link.to(ins, g.s_cm, l + 1)
                for c, (br, h) in enumerate(combos()):
                    v.wait_ge(g.s_sc, l * 12 + c + 1)
                    if c >= 3:
                        v.wait_ge(g.s_tp, l * 12 + c - 2)
                    link(v.tensor_tensor(S[c % 3][:, 0:256], PS[:, c % 3, 0:256], bm[:, h, :], ALU.add))
                    link(v.tensor_tensor(S[c % 3][:, 256:384], PS[:, c % 3, 256:384], bm[:, h, 128:256], ALU.add))
                    link(v.tensor_reduce(st[:, 64 + 2 * c + 1:64 + 2 * c + 2], S[c % 3][:, 0:256], AX_X, ALU.max, negate=True))
                    link.to(v.tensor_reduce(st[:, 64 + 2 * c:64 + 2 * c + 1], S[c % 3][:, 256:384], AX_X, ALU.max, negate=True), g.s_sd, l * 12 + c + 1)
                v.wait_ge(g.s_ex, l * 12 + 12)
                link(v.reciprocal(st[:, 96:120], st[:, 96:120]))
                w24 = st[:, 96:120].rearrange("p (b h t) -> p b h t", b=2, h=NH)
                for br in range(2):
                    for t in range(TT):
                        link(v.tensor_tensor(w24[:, br, :, t], w24[:, br, :, t], gate[:, t, :, 1 + br], ALU.mult))
                v.wait_ge(g.s_pv, l * 12 + 12)
                link(v.tensor_tensor(tmp[:].rearrange("p (c d) -> p c d", d=HD), PS[:, 5:8, :].rearrange("p b (c d) -> p (b c) d", d=HD),
                                     st[:, 96:120].unsqueeze(2).broadcast_to([P, 24, HD]), ALU.mult))
                m5 = tmp[:].rearrange("p (b h t d) -> p b h t d", b=2, h=NH, t=TT)
                for br in range(2):
                    for t in range(TT):
                        o = mix[:, t, 384:768].rearrange("p (h d) -> p h d", d=HD)
                        ins = v.tensor_tensor(o, o, m5[:, br, :, t, :], ALU.add)
                        if br == 1 and t == 1:
                            link.to(ins, g.s_mix, l + 1)
                        else:
                            link(ins)
                v.wait_ge(g.s_mt, l + 1)
                evac_transposed(g.s_md, 0, None, l + 1)
                v.wait_ge(g.s_wo, l + 1)
                for b in range(4):
                    xs = x[:, b // 2, 512 * (b % 2):512 * (b % 2) + 512]
                    link(v.tensor_tensor(xs, xs, PS[:, 4 + b, :], ALU.add))
                norm_rows(g.s_xn2, l + 1)
                v.wait_ge(g.s_xt2, l + 1)
                evac_transposed(g.s_hd2, 0, PC_FFN, l + 1)
                v.wait_ge(g.s_ha2, l + 1)
                v.sem_inc(g.s_ld, 1)
                for i in range(FF_BLOCKS):
                    v.wait_ge(g.s_th, l * FF_BLOCKS + i + 1)
                    if i >= 2:
                        v.wait_ge(g.s_dn, l * FF_BLOCKS + i - 1)
                    gp, upp = PS[:, 4 + 2 * (i % 2), :], PS[:, 5 + 2 * (i % 2), :]
                    link(v.scalar_tensor_tensor(th_T[i % 2], th_T[i % 2], 1.0, gp, ALU.add, ALU.mult))
                    link.to(v.scalar_tensor_tensor(act_T[i % 2], th_T[i % 2], 0.5, upp, ALU.mult, ALU.mult), g.s_actv, l * FF_BLOCKS + i + 1)
                v.wait_ge(g.s_dn, l * FF_BLOCKS + FF_BLOCKS)
                for b in range(4):
                    xs = x[:, b // 2, 512 * (b % 2):512 * (b % 2) + 512]
                    link(v.tensor_tensor(xs, xs, PS[:, b, :], ALU.add))
            link.leave(DEPTH)
            v.sem_inc(g.s_ld, 1)
            v.wait_ge(g.r_par, 16)
            v.wait_ge(g.act2, ACT2["r_c"] + 1)
            link(v.tensor_scalar(cs[:, 0:8], cs[:, 0:8], 0.5, 0.5, ALU.mult, ALU.add))
            link(v.tensor_tensor(cs[:, 0:8], cs[:, 0:8], p2[:, Q_C:Q_C + 8], ALU.mult))
            link.to(v.tensor_copy(cs[:, 8:264].rearrange("p (k m) -> p k m", k=8), cs[:, 0:8].unsqueeze(2).broadcast_to([P, 8, 32])), g.dve2, DVE2["r_cs"] + 1)
            norm_rows(g.dve2, DVE2["r_xn"] + 1)
            v.wait_ge(g.act2, ACT2["u_dt"] + 1)
            link(v.tensor_tensor(s5v[:, MAG], p2[:, Q_LRE:Q_LRE + 16], s5v[:, DT], ALU.mult))
            link(v.tensor_tensor(s5v[:, ANG], p2[:, Q_LIM:Q_LIM + 16], s5v[:, DT], ALU.mult))
            link(v.tensor_scalar(s5v[:, T1], s5v[:, ANG], 1.0 / TWO_PI, ROUND, ALU.mult, ALU.add))
            link(v.tensor_scalar(s5v[:, T1], s5v[:, T1], -ROUND, None, ALU.add))
            link(v.scalar_tensor_tensor(s5v[:, ANG], s5v[:, T1], -TWO_PI_HI, s5v[:, ANG], ALU.mult, ALU.add))
            link(v.scalar_tensor_tensor(s5v[:, ANG], s5v[:, T1], -(TWO_PI - TWO_PI_HI), s5v[:, ANG], ALU.mult, ALU.add))
            link.to(v.tensor_scalar(s5v[:, ANG], s5v[:, ANG], -3.1415925, 3.1415925, ALU.max, ALU.min), g.dve2, DVE2["u_ang"] + 1)
            v.wait_ge(g.act2, ACT2["u_sin"] + 1)
            link(v.tensor_tensor(s5v[:, COS_], s5v[:, COS_], s5v[:, COS_], ALU.mult))
            link.to(v.tensor_scalar(s5v[:, COS_], s5v[:, COS_], -2.0, 1.0, ALU.mult, ALU.add), g.dve2, DVE2["u_cs"] + 1)
            link(v.tensor_tensor(s5v[:, ABR], s5v[:, MAG], s5v[:, COS_], ALU.mult))
            link(v.tensor_scalar(s5v[:, ABR], s5v[:, ABR], -1.0, None, ALU.add))
            link(v.tensor_tensor(s5v[:, ABI], s5v[:, MAG], s5v[:, SIN_], ALU.mult))
            lre, lim = p2[:, Q_LRE:Q_LRE + 16], p2[:, Q_LIM:Q_LIM + 16]
            link(v.tensor_tensor(s5v[:, T1], lre, lre, ALU.mult))
            link(v.tensor_tensor(s5v[:, T2], lim, lim, ALU.mult))
            link(v.tensor_tensor(s5v[:, T1], s5v[:, T1], s5v[:, T2], ALU.add))
            link(v.reciprocal(s5v[:, T1], s5v[:, T1]))
            link(v.tensor_tensor(s5v[:, FRE], s5v[:, ABR], lre, ALU.mult))
            link(v.tensor_tensor(s5v[:, T2], s5v[:, ABI], lim, ALU.mult))
            link(v.tensor_tensor(s5v[:, FRE], s5v[:, FRE], s5v[:, T2], ALU.add))
            link(v.tensor_tensor(s5v[:, FRE], s5v[:, FRE], s5v[:, T1], ALU.mult))
            link(v.tensor_tensor(s5v[:, FIM], s5v[:, ABI], lre, ALU.mult))
            link(v.tensor_tensor(s5v[:, T2], s5v[:, ABR], lim, ALU.mult))
            link(v.tensor_tensor(s5v[:, FIM], s5v[:, FIM], s5v[:, T2], ALU.subtract))
            link(v.tensor_tensor(s5v[:, FIM], s5v[:, FIM], s5v[:, T1], ALU.mult))
            link(v.tensor_scalar(s5v[:, GLB][:, 0:4], p2[:, Q_GLB:Q_GLB + 4], 0.5, None, ALU.mult))
            v.wait_ge(g.r_ssm, 16)
            cre, cim = (ssm[:, i, :].rearrange("p (j m) -> p j m", j=16) for i in (2, 3))
            fr, fi = (s5v[:, f].unsqueeze(2).broadcast_to([P, 16, 32]) for f in (FRE, FIM))
            t1, t2 = (hTf[:, 512 * i:512 * i + 512].rearrange("p (j m) -> p j m", j=16) for i in range(2))
            t3 = cneg.rearrange("p (j m) -> p j m", j=16)
            link(v.tensor_tensor(t1, cre, fr, ALU.mult))
            link(v.tensor_tensor(t2, cim, fi, ALU.mult))
            link(v.tensor_tensor(t1, t1, t2, ALU.subtract))
            link(v.tensor_tensor(t3, cre, fi, ALU.mult))
            link(v.tensor_tensor(t2, cim, fr, ALU.mult))
            link(v.scalar_tensor_tensor(t3, t3, -1.0, t2, ALU.mult, ALU.subtract))
            link(v.tensor_copy(cre, t1))
            link.to(v.tensor_scalar(cim, t1, -1.0, None, ALU.mult), g.dve2, DVE2["u_cm"] + 1)
            v.wait_ge(g.r_row, 48)
            for n in (4, 5, 10, 11):
                v.wait_ge(g.r_adc, n + 1)
                i = n % 2 + (2 if n > 5 else 0)
                gr = g_row[:, 512 * i:512 * i + 512]
                link(v.tensor_tensor(gr, gr, PS[:, 2 + i, :], ALU.add))
                link(v.tensor_tensor(gr, gr, post[:, 512 * i:512 * i + 512], ALU.mult))
            v.wait_ge(g.r_adc, 12)
            for i, (sh, sc, gain) in enumerate(((0, 8, Q_MPRE), (24, 32, Q_FPRE))):
                link(v.tensor_tensor(mc[:, 16 * i:16 * i + 8], PS[:, 6, sh:sh + 8], p2[:, Q_ADB + sh:Q_ADB + sh + 8], ALU.add))
                s = mc[:, 16 * i + 8:16 * i + 16]
                link(v.tensor_tensor(s, PS[:, 6, sc:sc + 8], p2[:, Q_ADB + sc:Q_ADB + sc + 8], ALU.add))
                ins = v.scalar_tensor_tensor(s, s, 1.0, p2[:, gain:gain + 8], ALU.add, ALU.mult)
                if i == 0:
                    link(ins)
                else:
                    link.to(ins, g.dve2, DVE2["r_mc"] + 1)

            def evac_2(first, done, value, col):
                for b in (0, 2):
                    for k in (0, 1):
                        c = 2 * b + k
                        ins = v.tensor_scalar(hT[:, c, :], PS[:, first + b, 256 * k:256 * k + 256], mc[:, col + 8 + c:col + 9 + c],
                                              mc[:, col + c:col + c + 1], ALU.mult, ALU.add)
                        if c == 5:
                            link.to(ins, done, value)
                        else:
                            link(ins)

            v.wait_ge(g.pe2, PE2["r_xt"] + 1)
            evac_2(4, g.dve2, DVE2["r_hd"] + 1, 0)
            v.wait_ge(g.pe2, PE2["r_u"] + 1)
            link.to(v.tensor_copy(uT.rearrange("p (b c) t -> p b (c t)", b=2), PS[:, 0:2, :]), g.dve2, DVE2["r_ue"] + 1)
            v.wait_ge(g.pe2, PE2["r_qk"] + 1)
            link(v.tensor_copy(qk2.rearrange("p (b c) t -> p b (c t)", b=2), PS[:, 2:4, :]))
            link.to(v.tensor_copy(alr, PS[0:16, 0, 0:256]), g.dve2, DVE2["r_qke"] + 1)
            v.wait_ge(g.pe2, PE2["r_al"] + 1)
            for p in range(2):
                link(v.tensor_scalar(la[:, 256 * p:256 * p + 256], PS[:, 1, 256 * p:256 * p + 256], p2[:, Q_BAL + p:Q_BAL + p + 1], None, ALU.add))
            link.to(v.scalar_tensor_tensor(lb, la, -1.0, la, ALU.mult, ALU.max), g.dve2, DVE2["r_z"] + 1)
            v.wait_ge(g.act2, ACT2["r_ln"] + 1)
            link(v.scalar_tensor_tensor(la, la, 0.0, lb, ALU.min, ALU.subtract))
            link(v.tensor_scalar(lb, la, 1.0 / 16.0, None, ALU.mult))
            for p in range(2):
                ins = v.tensor_tensor_scan(la[:, 256 * p:256 * p + 256], K[:, K_RST:K_RST + T], lb[:, 256 * p:256 * p + 256], 0.0, ALU.mult, ALU.add)
                if p == 0:
                    link(ins)
                else:
                    link.to(ins, g.dve2, DVE2["r_b"] + 1)
            v.wait_ge(g.act2, ACT2["r_e"] + 1)
            qf, kf = (qk2[:, 2 * i:2 * i + 2, :].rearrange("p c t -> p (c t)") for i in range(2))
            link(v.scalar_tensor_tensor(qf, qf, 0.125, eb, ALU.mult, ALU.mult))
            link(v.tensor_tensor(lb, lb, kf, ALU.mult))
            link.to(v.tensor_tensor(ee, ee, kf, ALU.mult), g.dve2, DVE2["r_qd"] + 1)
            link(v.memset(sct, 0.0))
            v.wait_ge(g.pe2, PE2["r_sc"] + 1)
            mask = K[:, K_GM:K_GM + P].bitcast(I32).unsqueeze(1).broadcast_to([P, 4, P])
            for b in range(2):
                ins = v.copy_predicated(sct[:, 4 * b:4 * b + 4, :], mask, PS[:, 4 + b, :].rearrange("p (c t) -> p c t", c=4))
                if b == 0:
                    link(ins)
                else:
                    link.to(ins, g.dve2, DVE2["r_scd"] + 1)
            v.wait_ge(g.pe2, PE2["r_dl"] + 1)
            link(v.tensor_copy(gst[:, 0, :], PS[:, 0, 0:256]))
            for c in (1, 2):
                for p in range(2):
                    o = 256 * p + 64 * c + 63
                    ins = v.scalar_tensor_tensor(gst[:, c, P * p:P * p + P], gst[:, c - 1, P * p:P * p + P], eb[:, o:o + 1],
                                                 PS[:, c, P * p:P * p + P], ALU.mult, ALU.add)
                    if c == 2 and p == 1:
                        link.to(ins, g.dve2, DVE2["r_st"] + 1)
                    else:
                        link(ins)
            v.wait_ge(g.act2, ACT2["r_osq"] + 1)
            link(v.tensor_reduce(st[:, 208:216], osq.rearrange("p (c d) -> p c d", c=8), AX_X, ALU.add))
            y = rsqrt(mean_eps(8, P), 8)
            v.wait_ge(g.act2, ACT2["r_sg"] + 1)
            link(v.tensor_scalar(sgate, sgate, 0.5, 0.5, ALU.mult, ALU.add))
            link(v.tensor_tensor(sgate, sgate, og, ALU.mult))
            link(v.tensor_tensor(osq.rearrange("p (b c d) -> p b c d", b=2, c=4), PS[:, 6:8, :].rearrange("p b (c d) -> p b c d", c=4),
                                 y.rearrange("p (b c) -> p b c", b=2).unsqueeze(3).broadcast_to([P, 2, 4, P]), ALU.mult))
            link(v.tensor_tensor(osq.rearrange("p (c d) -> p c d", c=8), osq.rearrange("p (c d) -> p c d", c=8),
                                 gla_g.unsqueeze(1).broadcast_to([P, 8, P]), ALU.mult))
            o5 = osq.rearrange("p (b c t d) -> p b c t d", b=2, c=2, t=2)
            for t in range(TT):
                for b in range(2):
                    dst = xn[:, t, 0:512].rearrange("p (c b d) -> p c b d", c=2, b=2)[:, :, b, :]
                    sg4 = sgate[:, t, :].rearrange("p (c b d) -> p c b d", c=2, b=2)[:, :, b, :]
                    ins = v.tensor_tensor(dst, o5[:, b, :, t, :], sg4, ALU.mult)
                    if t == 1 and b == 1:
                        link.to(ins, g.dve2, DVE2["r_go"] + 1)
                    else:
                        link(ins)
            for q in range(4):
                er, ei = (etab3[q % 3][:, i, :].rearrange("p (j t) -> p j t", j=4) for i in range(2))
                zr, zi, yr, yi = (zy[:, i, :].rearrange("p (j t) -> p j t", j=4) for i in range(4))
                pr = [pp[:, i, :].rearrange("p (j t) -> p j t", j=4) for i in range(4)]
                br_, bi_ = PS[:, 0:4, 0:256], PS[:, 0:4, 256:512]
                v.wait_ge(g.u_e, q + 1)
                v.wait_ge(g.u_bu, q + 1)
                link(v.tensor_tensor(zr, er, br_, ALU.mult))
                link(v.tensor_tensor(yr, ei, bi_, ALU.mult))
                link(v.tensor_tensor(zr, zr, yr, ALU.add))
                link(v.tensor_tensor(zi, er, bi_, ALU.mult))
                link.to(v.tensor_tensor(yi, ei, br_, ALU.mult), g.u_bd, q + 1)
                link(v.tensor_tensor(zi, zi, yi, ALU.subtract))
                for src, dst in ((zr, yr), (zi, yi)):
                    for j in range(4):
                        dec = s5v[:, MAG][:, 4 * q + j:4 * q + j + 1].broadcast_to([P, T])
                        ins = v.tensor_tensor_scan(dst[:, j, :], dec, src[:, j, :], 0.0, ALU.mult, ALU.add)
                        link(ins)
                if q > 0:
                    v.wait_ge(g.u_c, q)
                link(v.tensor_tensor(pr[0], er, yr, ALU.mult))
                link(v.tensor_tensor(pr[1], ei, yi, ALU.mult))
                link(v.tensor_tensor(pr[2], er, yi, ALU.mult))
                link.to(v.tensor_tensor(pr[3], ei, yr, ALU.mult), g.u_pd, q + 1)
            v.wait_ge(g.u_c, 4)
            for q in range(4):
                link(v.scalar_tensor_tensor(yT[:, q, :], uT[:, q, :], p2[:, Q_D + q:Q_D + q + 1], PS[:, 4 + q // 2, 256 * (q % 2):256 * (q % 2) + 256],
                                            ALU.mult, ALU.add))
            yf = yT.rearrange("p q t -> p (q t)")
            link(v.tensor_tensor(yw, yf, yf, ALU.mult))
            link(v.tensor_scalar(yw, yw, GELU_B, 1.0, ALU.mult, ALU.add))
            link.to(v.tensor_tensor(yw, yw, yf, ALU.mult), g.dve2, DVE2["u_g1"] + 1)
            v.wait_ge(g.act2, ACT2["u_g2"] + 1)
            link(v.tensor_scalar(yw, yw, 0.5, 0.5, ALU.mult, ALU.add))
            link.to(v.tensor_tensor(yf, yf, yw, ALU.mult), g.dve2, DVE2["u_yg"] + 1)
            v.wait_ge(g.act2, ACT2["u_sg"] + 1)
            link(v.tensor_scalar(yw, yw, 0.5, 0.5, ALU.mult, ALU.add))
            link.to(v.tensor_tensor(hT[:, 4:8, :].rearrange("p k t -> p (k t)"), yw, yf, ALU.mult), g.dve2, DVE2["u_out"] + 1)

            def add_normed(src, gains):
                link(v.tensor_copy(st[:, 208:210], st[:, 230:232]))
                y2 = rsqrt(mean_eps(2, D), 2)
                for t in range(TT):
                    link(v.scalar_tensor_tensor(tmp[:, 0:1024], src(t), y2[:, t:t + 1], gains, ALU.mult, ALU.mult))
                    link(v.tensor_tensor(x[:, t, :], x[:, t, :], tmp[:, 0:1024], ALU.add))

            v.wait_ge(g.act2, ACT2["r_ss"] + 1)
            add_normed(lambda t: PS[:, 2 + 2 * t:4 + 2 * t, :].rearrange("p b n -> p (b n)"), g_row[:, 0:1024])
            norm_rows(g.dve2, DVE2["r_xn3"] + 1)
            v.wait_ge(g.pe2, PE2["r_xt3"] + 1)
            evac_2(4, g.dve2, DVE2["r_hd3"] + 1, 16)
            v.wait_ge(g.pe2, PE2["r_xb"] + 1)
            for b in (0, 2):
                ins = v.tensor_copy(xn[:, b // 2, 512 * (b % 2):512 * (b % 2) + 512], PS[:, b, :])
                if b == 0:
                    link(ins)
                else:
                    link.to(ins, g.dve2, DVE2["r_xbd"] + 1)
            v.wait_ge(g.pe2, PE2["m_lg"] + 1)
            lg = mst[:, 16:80].rearrange("p (t e) -> p t e", t=TT)
            link(v.tensor_tensor(lg, PS[:, 4, 0:64].rearrange("p (t e) -> p t e", t=TT), p2[:, Q_RB:Q_RB + 32].unsqueeze(1).broadcast_to([P, TT, 32]), ALU.add))
            for t in range(TT):
                link(v.max(mst[:, 80 + 8 * t:88 + 8 * t], lg[:, t, :]))
                link(v.max_index(mix_i[:, 8 * t:8 * t + 8], mst[:, 80 + 8 * t:88 + 8 * t], lg[:, t, :]))
                link(v.tensor_scalar(mst[:, 4 * t:4 * t + 4], mst[:, 80 + 8 * t:84 + 8 * t], mst[:, 80 + 8 * t:81 + 8 * t], None, ALU.subtract))
            link.to(v.tensor_copy(mst[:, 96:112], mix_i), g.dve2, DVE2["m_top"] + 1)
            v.wait_ge(g.act2, ACT2["m_exp"] + 1)
            top = mst[:, 0:8].rearrange("p (t k) -> p t k", t=TT)
            link(v.tensor_reduce(mst[:, 8:10], top, AX_X, ALU.add))
            link(v.reciprocal(mst[:, 8:10], mst[:, 8:10]))
            link(v.tensor_tensor(top, top, mst[:, 8:10].unsqueeze(2).broadcast_to([P, TT, 4]), ALU.mult))
            for t in range(TT):
                for k in range(4):
                    hot = oh2
                    idx, gk = mst[:, 96 + 8 * t + k:97 + 8 * t + k], mst[:, 4 * t + k:4 * t + k + 1]
                    if k == 0:
                        link(v.tensor_scalar(gates[:, t, :], K[:, K_E32:K_E32 + 32], idx, gk, ALU.is_equal, ALU.mult))
                        link(v.tensor_scalar(chosen[:, t, :], K[:, K_E32:K_E32 + 32], idx, None, ALU.is_equal))
                    else:
                        link(v.tensor_scalar(hot, K[:, K_E32:K_E32 + 32], idx, None, ALU.is_equal))
                        link(v.scalar_tensor_tensor(gates[:, t, :], hot, gk, gates[:, t, :], ALU.mult, ALU.add))
                        link(v.tensor_tensor(chosen[:, t, :], chosen[:, t, :], hot, ALU.add))
            v.sem_inc(g.dve2, 1)
            v.wait_ge(g.pe2, PE2["m_rk"] + 1)
            rk = PS[:, 5, 0:64].rearrange("p (t e) -> p t e", t=TT)
            link(v.scalar_tensor_tensor(rank, rk, 1.0, chosen, ALU.add, ALU.mult))
            link(v.tensor_scalar(rank, rank, -1.0, None, ALU.add))
            more, ends = mst[:, 112:128], tmp[:, 0:32]
            link(v.tensor_scalar(ends, PS[:, 5, 64:96], 64.5, None, ALU.is_gt))
            for lim_ in (128.5, 192.5):
                link(v.scalar_tensor_tensor(ends, PS[:, 5, 64:96], lim_, ends, ALU.is_gt, ALU.add))
            link(v.tensor_tensor_scan(tmp[:, 32:64], K[:, K_ONE:K_ONE + 32], ends, 0.0, ALU.mult, ALU.add))
            below = tmp[:, 64:576].rearrange("p (j e) -> p j e", j=16)
            link(v.tensor_tensor(below, tmp[:, 32:64].unsqueeze(1).broadcast_to([P, 16, 32]), K[:, K_E32:K_E32 + 16].unsqueeze(2).broadcast_to([P, 16, 32]), ALU.is_le))
            link(v.tensor_reduce(more, below, AX_X, ALU.add))
            link(v.tensor_scalar(more, more, float(N_EXPERTS - 1), None, ALU.min))
            link(v.tensor_scalar(tmp[:, 63:64], tmp[:, 63:64], float(N_EXPERTS), None, ALU.add))
            link(v.tensor_copy(item_i[:, 0:32], K[:, K_E32:K_E32 + 32]))
            link(v.tensor_copy(item_i[:, 32:48], more))
            link(v.tensor_copy(item_i[:, 48:49], more[:, 15:16]))
            link(v.tensor_copy(gT, PS[0:32, 6, 0:256]))
            link.to(v.tensor_copy(item_i[:, 63:64], tmp[:, 63:64]), g.dve2, DVE2["m_rounds"] + 1)
            v.wait_ge(g.pe2, PE2["m_bd"] + 1)
            for b in range(4):
                link(v.tensor_copy(oacc[:, b // 2, 512 * (b % 2):512 * (b % 2) + 512], PS[:, b, :]))
            v.sem_inc(g.dve2, 1)

            def hot_rows(ch, e, value):
                for t in range(TT):
                    ch(v.tensor_scalar(hot1[:, t, :], K[:, K_IOTA:K_IOTA + P], rank[:, t, bass.ds(e, 1)], None, ALU.is_equal))
                for t in range(TT):
                    ins = v.tensor_scalar(hotw[:, t, :], K[:, K_IOTA:K_IOTA + P], rank[:, t, bass.ds(e, 1)], gates[:, t, bass.ds(e, 1)], ALU.is_equal, ALU.mult)
                    if t == 0:
                        ch(ins)
                    else:
                        ch.to(ins, g.m_p, value)
                for t in range(TT):
                    ch(v.tensor_scalar(rank[:, t, bass.ds(e, 1)], rank[:, t, bass.ds(e, 1)], -64.0, None, ALU.add))

            def expert_row(ch, e, value):
                ch.to(v.tensor_scalar(esel, K[0:32, K_ONE:K_ONE + 64], ident[0:32, bass.ds(e, 1)], None, ALU.mult), g.m_es, value)

            items = v.value_load(item_i[0:1, 63:64], min_val=N_EXPERTS, max_val=N_EXPERTS + 16)
            v.sem_inc(g.m_sd, 1)
            ch = Link(v, g.m_dve)
            first = v.value_load(item_i[0:1, 0:1], min_val=0, max_val=N_EXPERTS - 1)
            hot_rows(ch, first, 1)
            expert_row(ch, first, 1)
            v.wait_ge(g.m_pw, 1)
            ch.to(v.tensor_copy(pwT, PS[:, 5, 0:256]), g.m_pwe, 1)
            with v.Fori(0, items) as n:
                ch.enter(n, MOE_STEPS)
                after = v.value_load(item_i[0:1, bass.ds(n + 1, 1)], min_val=0, max_val=N_EXPERTS - 1)
                v.wait_ge(g.m_pw, n + 1)
                hot_rows(ch, after, n + 2)
                v.wait_ge(g.m_gu, n + 1)
                ch.to(v.tensor_scalar(mgs, PS[:, 0, :], SWIGLU_LIMIT, None, ALU.min), g.m_gs, n + 1)
                ch(v.tensor_scalar(mus, PS[:, 1, :], SWIGLU_LIMIT, -SWIGLU_LIMIT, ALU.min, ALU.max))
                v.wait_ge(g.m_th, n + 1)
                ch(v.scalar_tensor_tensor(mth, mth, 1.0, mgs, ALU.add, ALU.mult))
                ch.to(v.scalar_tensor_tensor(mus, mus, 1.0, mth, ALU.add, ALU.mult), g.m_a, n + 1)
                expert_row(ch, after, n + 2)
                for t in range(TT):
                    v.wait_ge(g.m_s, 2 * n + t + 1)
                    for h in range(2):
                        o = oacc[:, t, 512 * h:512 * h + 512]
                        ins = v.tensor_tensor(o, o, PS[:, (6 + h, 3 + h)[t], :], ALU.add)
                        if h == 0:
                            ch(ins)
                        else:
                            ch.to(ins, g.m_sd, 2 * n + t + 2)
                    if t == 0:
                        v.wait_ge(g.m_s, 2 * n + 2)
                        v.wait_ge(g.m_pw, n + 2)
                        ch.to(v.tensor_copy(pwT, PS[:, 5, 0:256]), g.m_pwe, n + 2)
            assert ch.n == MOE_STEPS, ch.n
            for t in range(TT):
                v.tensor_tensor_reduce(tmp2, oacc[:, t, :], oacc[:, t, :], 1.0, 0.0, ALU.mult, ALU.add, st[:, 230 + t:231 + t]).then_inc(g.m_f, 1)
                v.wait_ge(g.m_f, t + 1)
            add_normed(lambda t: oacc[:, t, :], g_row[:, 1024:2048])
            v.sem_inc(g.dve2, 1)

        @block.tensor
        def _(pe):
            def arrived(key, l):
                slot, use = PLACE[key]
                pe.wait_ge(landed[slot], (l * SLOT_USES[slot] + use) * 16 + 16)
                return ring[:, slot, :]

            def release(key, ins):
                ins.then_inc(freed[PLACE[key][0]], 1)

            def transposes(src, first, done):
                for c in range(KC):
                    for t in range(TT):
                        ins = pe.transpose(PS[:, first + c // 2, 256 * (c % 2) + 128 * t:256 * (c % 2) + 128 * t + 128],
                                           src[:, t, 128 * c:128 * c + 128], ident)
                ins.then_inc(done, 1)

            for s in range(RING):
                pe.sem_inc(freed[s], 1)
            pe.wait_ge(g.s_oh, 32)
            oh = tb[0:WIN_BUCKETS, 0, 0:9, :].rearrange("p a b -> p (a b)")
            pe.matmul(PS[0:NH, 0, :], kc[0:WIN_BUCKETS, 0, 0:NH], oh[:, 0:512], start=True, stop=True).then_inc(g.s_b3, 1)
            pe.wait_ge(g.s_b2, 16)
            pe.wait_ge(g.s_k, 16)
            for i in range(3):
                ins = pe.matmul(PS[:, 1 + i, :], K[:, K_FLIP:K_FLIP + P], proj[:, 0, 512 * i:512 * i + 512], start=True, stop=True)
            ins.then_inc(g.s_b4, 1)
            with pe.Fori(0, DEPTH) as l:
                pe.wait_ge(g.s_xn, l + 1)
                transposes(xn, 4, g.s_xt)
                pe.wait_ge(g.s_hd, l + 1)
                pe.wait_ge(g.s_ha, l + 1)
                for nb in range(WIN_BLOCKS):
                    w = 512 if nb < WIN_BLOCKS - 1 else WIN_LAST
                    wt = arrived(("win", nb), l)[:, 0:KC * w].rearrange("p (k n) -> p k n", k=KC)
                    if nb >= 4:
                        pe.wait_ge(g.s_pd, l * 7 + nb - 3)
                        pe.wait_ge(g.s_pa, l * 7 + nb - 3)
                    for t in range(TT):
                        for k in range(KC):
                            ins = pe.matmul(PS[:, (2 * nb + t) % 8, 0:w], hT[:, k, 128 * t:128 * t + 128], wt[:, k, :], start=k == 0, stop=k == KC - 1)
                        ins.then_inc(g.s_pj, 1)
                    pe.wait_ge(g.s_pj, l * 14 + 2 * nb + 2)
                    pe.sem_inc(freed[PLACE[("win", nb)][0]], 1)
                pe.wait_ge(g.s_pd, l * 7 + 7)
                pe.wait_ge(g.s_pa, l * 7 + 7)
                for j in range(2):
                    for t in range(TT):
                        ins = pe.transpose(PS[:, 6, 256 * j + 128 * t:256 * j + 128 * t + 128], proj[:, t, NKV + 128 * j:NKV + 128 * j + 128], ident)
                ins.then_inc(g.s_t0, 1)
                pe.wait_ge(g.s_rope, l + 1)
                for c in range(6):
                    for t in range(TT):
                        ins = pe.transpose(PS[:, c // 2, 256 * (c % 2) + 128 * t:256 * (c % 2) + 128 * t + 128], tb[:, t, c, :], ident)
                ins.then_inc(g.s_t1, 1)
                pe.wait_ge(g.s_nk, l + 1)
                for c in range(5):
                    for t in range(TT):
                        ins = pe.transpose(PS[:, 3 + c // 2, 256 * (c % 2) + 128 * t:256 * (c % 2) + 128 * t + 128], tb[:, t, 6 + c, :], ident)
                ins.then_inc(g.s_t2, 1)
                pe.wait_ge(g.s_e3, l + 1)
                cw1 = arrived(("cw1", 0), l)[:, 0:2048].rearrange("p (j m e) -> p j m e", j=2, m=16)
                for j in range(2):
                    bj = blocks[:, j, :, :].rearrange("p g (i m) -> p (g i) m", m=16)
                    for m in range(16):
                        ins = pe.matmul(PS[0:64, 7, 30 * j:30 * j + 30], cw1[:, j, m, :], bj[:, :, m], start=m == 0, stop=m == 15)
                ins.then_inc(g.s_c1, 1)
                pe.wait_ge(g.s_c1, l + 1)
                pe.sem_inc(freed[PLACE[("cw1", 0)][0]], 1)
                pe.wait_ge(g.s_e1, l + 1)

                def ret_scores(h):
                    rows = slice(64 * (h % 2), 64 * (h % 2) + 64)
                    if h >= 3:
                        pe.wait_ge(g.s_rd, l * NH + h - 2)
                    q, kk = tT[rows, h // 2, :], tT[rows, 3 + h // 2, :]
                    pe.matmul(PS[:, h % 3, 0:256], kk[:, 0:128], q, start=True, stop=True)
                    pe.matmul(PS[:, h % 3, 256:384], kk[:, 128:256], q[:, 128:256], start=True, stop=True).then_inc(g.s_rs, 1)

                def ret_out(h):
                    pe.wait_ge(g.s_rd, l * NH + h + 1)
                    if h == 0:
                        pe.wait_ge(g.s_e2, l + 1)
                    vh = proj[:, :, RV + HD * h:RV + HD * (h + 1)]
                    s = S[h % 3]
                    pe.matmul(PS[:, 3, HD * h:HD * h + HD], s[:, 0:128], vh[:, 0, :], start=True, stop=True)
                    pe.matmul(PS[:, 4, HD * h:HD * h + HD], s[:, 128:256], vh[:, 0, :], start=True, stop=False)
                    ins = pe.matmul(PS[:, 4, HD * h:HD * h + HD], s[:, 256:384], vh[:, 1, :], start=False, stop=True)
                    ins.then_inc(g.s_rp2, 1)

                for h in range(NH + 1):
                    if h < NH:
                        ret_scores(h)
                    if h >= 1:
                        ret_out(h - 1)
                pe.wait_ge(g.s_rp2, l * NH + NH)
                pe.sem_inc(g.s_rp, 1)
                pe.wait_ge(g.s_g3, l + 1)
                for gr in range(4):
                    ins = pe.matmul(PS[:, 5, 128 * gr:128 * gr + 128].rearrange("p (c d) -> p c d", c=TT), par[:, PC_WS + 128 * gr:PC_WS + 128 * gr + 128],
                                    proj[:, :, GM + 256 + 64 * gr:GM + 320 + 64 * gr], start=True, stop=True)
                ins.then_inc(g.s_gp, 1)
                pe.wait_ge(g.s_c4, l + 1)
                pe.sem_inc(g.s_pe, 1)
                w2 = par[0:64, PC_W2:PC_W2 + 128].rearrange("p (j e) -> p j e", j=2)
                pe.matmul(PS[0:30, 7, 0:64], hid[:, 2, 0:30], w2[:, 0, :], start=True, stop=True)
                for gr in range(2):
                    ins = pe.matmul(PS[0:NCMP, 7, 64 + 64 * gr:128 + 64 * gr], hid[:, 2, 30 + 15 * gr:45 + 15 * gr], w2[:, 1, :], start=True, stop=True)
                ins.then_inc(g.s_c5, 1)
                pe.wait_ge(g.s_c6, l + 1)
                pe.sem_inc(g.s_pe, 1)
                pe.transpose(PS[:, 7, 0:30], kc[0:30, 2, :], ident[0:30, 0:30]).then_inc(g.s_c7, 1)
                pe.wait_ge(g.s_c8, l + 1)
                for h in range(NH):
                    rows = slice(64 * (h % 2), 64 * (h % 2) + 64)
                    for t in range(TT):
                        o = 15 * (3 * t + h // 2)
                        ins = pe.matmul(PS[:, 7 - h % 2, o:o + 15], tT[rows, 6 + h // 2, 128 * t:128 * t + 128], kcT[rows, 15 * (h // 3):15 * (h // 3) + 15],
                                        start=True, stop=True)
                ins.then_inc(g.s_c9, 1)
                pe.wait_ge(g.s_c12, l + 1)
                for c in range(12):
                    ins = pe.transpose(PS[0:NCMP, c // 4, 128 * (c % 4):128 * (c % 4) + 128], pcm[:, c // 6, c % 6, :], ident)
                ins.then_inc(g.s_c13, 1)
                pe.wait_ge(g.s_c14, l + 1)
                for c in range(12):
                    h = c % 6
                    ins = pe.matmul(PS[:, 6 + c // 6, HD * h:HD * h + HD], pcT[:, c, :], vc[:, 64 * (h // 3):64 * (h // 3) + 64], start=True, stop=True)
                ins.then_inc(g.s_c15, 1)

                def scores(c):
                    br, h = combos()[c]
                    rows = slice(64 * (h % 2), 64 * (h % 2) + 64)
                    if c >= 3:
                        pe.wait_ge(g.s_sd, l * 12 + c - 2)
                    q, kk = tT[rows, 6 + h // 2, :], tT[rows, 9 + 2 * br + h // 3, :]
                    pe.matmul(PS[:, c % 3, 0:256], q[:, 128:256], kk, start=True, stop=True)
                    pe.matmul(PS[:, c % 3, 256:384], q[:, 0:128], kk[:, 0:128], start=True, stop=True).then_inc(g.s_sc, 1)

                def turn(c):
                    pe.wait_ge(g.s_ex, l * 12 + c + 1)
                    if c == 0:
                        pe.wait_ge(g.s_rm, l + 1)
                    if c >= 2:
                        pe.wait_ge(g.s_pe2, l * 12 + c - 1)
                    for b in range(3):
                        ins = pe.transpose(PS[:, 3 + c % 2, 128 * b:128 * b + 128], S[c % 3][:, 128 * b:128 * b + 128], ident)
                    ins.then_inc(g.s_tp, 1)

                def values(c):
                    br, h = combos()[c]
                    pe.wait_ge(g.s_pe2, l * 12 + c + 1)
                    if c == 0:
                        pe.wait_ge(g.s_cm, l + 1)
                    o = NKV + 256 * (1 + br) + 128 + 64 * (h // 3)
                    ov = PS[:, 5 + c // 4, 128 * (c % 4):128 * (c % 4) + 128]
                    pe.matmul(ov[:, 0:64], PT[c % 2][:, 256:384], proj[:, 0, o:o + 64], start=True, stop=True)
                    pe.matmul(ov[:, 64:128], PT[c % 2][:, 0:128], proj[:, 0, o:o + 64], start=True, stop=False)
                    pe.matmul(ov[:, 64:128], PT[c % 2][:, 128:256], proj[:, 1, o:o + 64], start=False, stop=True).then_inc(g.s_pv, 1)

                for i in range(14):
                    if i < 12:
                        scores(i)
                    if 1 <= i <= 12:
                        turn(i - 1)
                    if i >= 2:
                        values(i - 2)
                pe.wait_ge(g.s_mix, l + 1)
                transposes(mix, 0, g.s_mt)
                pe.wait_ge(g.s_md, l + 1)
                pe.wait_ge(g.s_ma, l + 1)
                for nh in range(2):
                    wt = arrived(("wout", nh), l).rearrange("p (k n) -> p k n", k=KC)
                    for t in range(TT):
                        for k in range(KC):
                            ins = pe.matmul(PS[:, 4 + 2 * t + nh, :], hT[:, k, 128 * t:128 * t + 128], wt[:, k, :], start=k == 0, stop=k == KC - 1)
                    if nh == 0:
                        release(("wout", 0), ins)
                ins.then_inc(g.s_wo, 1)
                pe.wait_ge(g.s_wo, l + 1)
                pe.sem_inc(freed[PLACE[("wout", 1)][0]], 1)
                pe.wait_ge(g.s_xn2, l + 1)
                transposes(xn, 0, g.s_xt2)
                pe.wait_ge(g.s_hd2, l + 1)
                pe.wait_ge(g.s_ha2, l + 1)
                for i in range(FF_BLOCKS + 1):
                    if i < FF_BLOCKS:
                        wt = arrived(("gu", i), l).rearrange("p (k n) -> p k n", k=KC)
                        if i >= 2:
                            pe.wait_ge(g.s_actv, l * FF_BLOCKS + i - 1)
                        for part in range(2):
                            for f in range(2):
                                for k in range(KC):
                                    ins = pe.matmul(PS[:, 4 + 2 * (i % 2) + part, 256 * f:256 * f + 256], wt[:, k, 256 * part + 128 * f:256 * part + 128 * f + 128],
                                                    hT[:, k, :], start=k == 0, stop=k == KC - 1)
                        ins.then_inc(g.s_gu, 1)
                        pe.wait_ge(g.s_gu, l * FF_BLOCKS + i + 1)
                        pe.sem_inc(freed[PLACE[("gu", i)][0]], 1)
                    if i >= 1:
                        c = i - 1
                        wd = arrived(("dn", c // 2), l).rearrange("p (f n) -> p f n", f=4)
                        pe.wait_ge(g.s_actv, l * FF_BLOCKS + c + 1)
                        for t in range(TT):
                            for nh in range(2):
                                for f in range(2):
                                    ft = 2 * c + f
                                    ins = pe.matmul(PS[:, 2 * t + nh, :], act_T[c % 2][:, 256 * f + 128 * t:256 * f + 128 * t + 128],
                                                    wd[:, ft % 4, 512 * nh:512 * nh + 512], start=ft == 0, stop=ft == FF_TILES - 1)
                        ins.then_inc(g.s_dn, 1)
                        if c % 2 == 1 or c == FF_BLOCKS - 1:
                            pe.wait_ge(g.s_dn, l * FF_BLOCKS + c + 1)
                            pe.sem_inc(freed[PLACE[("dn", c // 2)][0]], 1)
            def land_2(key):
                slot, load, use = PLACE_2[key]
                pe.wait_ge(landed[slot], 16 * load + 16)
                return ring[:, slot, :]

            pe.wait_ge(g.dve2, DVE2["r_cs"] + 1)
            pe.wait_ge(g.r_par, 16)
            for n in range(12):
                wt = land_2(("ada", n)).rearrange("p (k n) -> p k n", k=KC)
                if n >= 2:
                    pe.wait_ge(g.act2, ACT2["r_ade"] + n - 1)
                for k in range(KC):
                    j = k % 4
                    ins = pe.matmul(PS[32 * j:32 * j + 32, n % 2, :], cs[:, 8 + 32 * k:40 + 32 * k], wt[:, k, :], start=k < 4, stop=k >= 4,
                                    skip_group_check=True)
                ins.then_inc(g.r_ada, 1)
                pe.wait_ge(g.r_ada, n + 1)
                pe.sem_inc(freed[PLACE_2[("ada", n)][0]], 1)
                pe.wait_ge(g.act2, ACT2["r_ade"] + n + 1)
                if n in (4, 5, 10, 11):
                    i = n % 2 + (2 if n > 5 else 0)
                    ins = pe.matmul(PS[:, 2 + i, :], K[:, K_SEL:K_SEL + P], modr[n % 2], start=True, stop=True)
                else:
                    for c in range(4):
                        ins = pe.matmul(PS[:, 6, 4 * n + c:4 * n + c + 1], modr[n % 2][:, P * c:P * c + P], K[:, K_SEL:K_SEL + 1], start=True, stop=True)
                ins.then_inc(g.r_adc, 1)
            pe.wait_ge(g.dve2, DVE2["r_mc"] + 1)
            pe.wait_ge(g.dve2, DVE2["r_xn"] + 1)
            transposes(xn, 4, g.pe2)
            pe.wait_ge(g.dve2, DVE2["r_hd"] + 1)
            pe.wait_ge(g.act2, ACT2["r_ha"] + 1)

            def transposed(key, first, done, value):
                wt = land_2(key).rearrange("p (k n) -> p k n", k=KC)
                for f in range(4):
                    for k in range(KC):
                        ins = pe.matmul(PS[:, first + f // 2, 256 * (f % 2):256 * (f % 2) + 256], wt[:, k, P * f:P * f + P], hT[:, k, :],
                                        start=k == 0, stop=k == KC - 1)
                ins.then_inc(done, 1)
                pe.wait_ge(done, value)
                pe.sem_inc(freed[PLACE_2[key][0]], 1)

            transposed(("win2", 0), 0, g.pe2, PE2["r_u"] + 1)
            transposed(("win2", 1), 2, g.pe2, PE2["r_qk0"] + 1)
            pe.wait_ge(g.dve2, DVE2["r_ue"] + 1)
            wl = p2[:, Q_WL:Q_WL + 128].rearrange("p (k n) -> p k n", k=KC)
            for k in range(KC):
                ins = pe.matmul(PS[0:16, 0, 0:256], wl[:, k, :], hT[:, k, :], start=k == 0, stop=k == KC - 1)
            ins.then_inc(g.pe2, 1)
            for b in range(2):
                wt = land_2(("win2", 2 + b)).rearrange("p (k n) -> p k n", k=KC)
                for t in range(TT):
                    for k in range(KC):
                        ins = pe.matmul(PS[:, 4 + 2 * b + t, :], hT[:, k, P * t:P * t + P], wt[:, k, :], start=k == 0, stop=k == KC - 1)
                    ins.then_inc(g.pe2, 1)
                pe.wait_ge(g.pe2, PE2["r_vo"] + 2 * b + 2)
                pe.sem_inc(freed[PLACE_2[("win2", 2 + b)][0]], 1)
            pe.wait_ge(g.dve2, DVE2["r_qke"] + 1)
            for p in range(2):
                ins = pe.matmul(PS[:, 1, 256 * p:256 * p + 256], p2[0:16, Q_WA + P * p:Q_WA + P * p + P], alr, start=True, stop=True)
            ins.then_inc(g.pe2, 1)
            pe.wait_ge(g.dve2, DVE2["r_qd"] + 1)
            for t in range(TT):
                for p in range(2):
                    ins = pe.transpose(PS[:, 2, 256 * t + P * p:256 * t + P * p + P], ee[:, 256 * p + P * t:256 * p + P * t + P], ident)
            ins.then_inc(g.pe2, 1)
            pe.wait_ge(g.act2, ACT2["r_voe"] + 4)
            for h in range(4):
                rows = slice(64 * (h % 2), 64 * (h % 2) + 64)
                for t in range(TT):
                    o = 256 * (h // 2) + P * t
                    ins = pe.matmul(PS[:, 4 + h % 2, o:o + P], lb[rows, o:o + P], qk2[rows, h // 2, P * t:P * t + P], start=True, stop=True)
            ins.then_inc(g.pe2, 1)
            pe.wait_ge(g.act2, ACT2["r_kee"] + 1)
            for c in range(3):
                rows = slice(64 * (c % 2), 64 * (c % 2) + 64)
                for h in range(4):
                    ins = pe.matmul(PS[64 * (h % 2):64 * (h % 2) + 64, c, P * (h // 2):P * (h // 2) + P], ke[rows, c // 2, 64 * h:64 * h + 64],
                                    vv2[rows, c // 2, P * h:P * h + P], start=True, stop=True)
            ins.then_inc(g.pe2, 1)
            pe.wait_ge(g.dve2, DVE2["r_scd"] + 1)
            pe.wait_ge(g.dve2, DVE2["r_st"] + 1)
            for h in range(4):
                rows = slice(64 * (h % 2), 64 * (h % 2) + 64)
                for t in range(TT):
                    o = 256 * (h // 2) + P * t
                    pe.matmul(PS[:, 6 + h % 2, o:o + P], sct[:, 4 * (h % 2) + 2 * (h // 2) + t, :], vv2[:, t, P * h:P * h + P],
                              start=True, stop=False, skip_group_check=True)
                    for cc in range(2):
                        c = 2 * t + cc
                        if c > 0:
                            ins = pe.matmul(PS[64 * cc:64 * cc + 64, 6 + h % 2, o:o + P], qk2[rows, h // 2, 64 * c:64 * c + 64],
                                            gst[rows, c - 1, P * (h // 2):P * (h // 2) + P], start=False, stop=True, skip_group_check=True)
            ins.then_inc(g.pe2, 1)

            def inputs(q):
                for j in range(4):
                    rows = slice(32 * j, 32 * j + 32)
                    for i in range(2):
                        ins = pe.matmul(PS[:, j, 256 * i:256 * i + 256], ssm[rows, i, P * q:P * q + P], uT[rows, q, :], start=True, stop=True)
                ins.then_inc(g.u_bu, 1)

            def outputs(q):
                pe.wait_ge(g.u_pd, q + 1)
                for j in range(4):
                    cols = slice(P * q + 32 * j, P * q + 32 * j + 32)
                    for i, mat in enumerate((ssm[:, 2, cols], ssm[:, 3, cols], cneg[:, cols], cneg[:, cols])):
                        ins = pe.matmul(PS[32 * j:32 * j + 32, 4 + q // 2, 256 * (q % 2):256 * (q % 2) + 256], mat, pp[:, i, 256 * j:256 * j + 256],
                                        start=i == 0, stop=i == 3, skip_group_check=True)
                ins.then_inc(g.u_c, 1)

            pe.wait_ge(g.dve2, DVE2["r_st"] + 1)
            pe.wait_ge(g.r_ssm, 16)
            inputs(0)
            pe.wait_ge(g.dve2, DVE2["r_go"] + 1)
            for c in range(4):
                for t in range(TT):
                    ins = pe.transpose(PS[:, 6 + c // 2, 256 * (c % 2) + P * t:256 * (c % 2) + P * t + P], xn[:, t, P * c:P * c + P], ident)
            ins.then_inc(g.pe2, 1)
            pe.wait_ge(g.dve2, DVE2["u_cm"] + 1)
            for q in range(4):
                if q < 3:
                    pe.wait_ge(g.u_bd, q + 1)
                    inputs(q + 1)
                outputs(q)
            pe.wait_ge(g.u_c, 4)
            for s in (3, 4, 5):
                pe.sem_inc(freed[s], 1)
            pe.wait_ge(g.dve2, DVE2["u_yg"] + 1)
            pe.wait_ge(g.u_bd, 4)
            wt = land_2(("glu", 0))[:, 0:2048].rearrange("p (k n) -> p k n", k=4)
            for f in range(4):
                for k in range(4):
                    ins = pe.matmul(PS[:, f // 2, 256 * (f % 2):256 * (f % 2) + 256], wt[:, k, P * f:P * f + P], yT[:, k, :], start=k == 0, stop=k == 3)
            ins.then_inc(g.pe2, 1)
            pe.wait_ge(g.pe2, PE2["u_glu"] + 1)
            pe.sem_inc(freed[PLACE_2[("glu", 0)][0]], 1)
            pe.wait_ge(g.act2, ACT2["r_ote"] + 1)
            pe.wait_ge(g.dve2, DVE2["u_out"] + 1)
            for nh in range(2):
                wt = land_2(("wout2", nh)).rearrange("p (k n) -> p k n", k=KC)
                for t in range(TT):
                    for k in range(KC):
                        ins = pe.matmul(PS[:, 2 + 2 * t + nh, :], hT[:, k, P * t:P * t + P], wt[:, k, :], start=k == 0, stop=k == KC - 1)
                if nh == 0:
                    ins.then_inc(freed[PLACE_2[("wout2", 0)][0]], 1)
            ins.then_inc(g.pe2, 1)
            pe.wait_ge(g.pe2, PE2["r_wo"] + 1)
            pe.sem_inc(freed[PLACE_2[("wout2", 1)][0]], 1)
            pe.wait_ge(g.dve2, DVE2["r_xn3"] + 1)
            transposes(xn, 4, g.pe2)
            pe.wait_ge(g.dve2, DVE2["r_hd3"] + 1)
            pe.wait_ge(g.act2, ACT2["r_ha3"] + 1)
            for t in range(TT):
                for k in range(KC):
                    ins = pe.transpose(PS[:, 2 * t + k // 4, P * (k % 4):P * (k % 4) + P], hT[:, k, P * t:P * t + P], ident)
            ins.then_inc(g.pe2, 1)
            rw = p2[:, Q_RW:Q_RW + 256].rearrange("p (k n) -> p k n", k=KC)
            for t in range(TT):
                for k in range(KC):
                    ins = pe.matmul(PS[:, 4, 32 * t:32 * t + 32], hT[:, k, P * t:P * t + P], rw[:, k, :], start=k == 0, stop=k == KC - 1)
            ins.then_inc(g.pe2, 1)
            pe.wait_ge(g.dve2, DVE2["m_ch"] + 1)
            sut, one = K[:, K_SUT:K_SUT + P], K[:, K_ONE:K_ONE + P]
            pe.matmul(PS[:, 5, 0:32], sut, chosen[:, 0, :], start=True, stop=True)
            pe.matmul(PS[:, 5, 32:64], one, chosen[:, 0, :], start=True, stop=False)
            pe.matmul(PS[:, 5, 32:64], sut, chosen[:, 1, :], start=False, stop=True)
            pe.matmul(PS[:, 5, 64:96], one, chosen[:, 0, :], start=True, stop=False)
            pe.matmul(PS[:, 5, 64:96], one, chosen[:, 1, :], start=False, stop=True)
            for t in range(TT):
                ins = pe.transpose(PS[0:32, 6, P * t:P * t + P], gates[:, t, :], ident)
            ins.then_inc(g.pe2, 1)
            pe.wait_ge(g.dve2, DVE2["m_rounds"] + 1)
            pe.wait_ge(g.dve2, DVE2["r_xbd"] + 1)
            pe.wait_ge(g.act2, ACT2["r_xbe"] + 1)
            for b in range(4):
                ins = pe.matmul(PS[:, b, :], gT[:, P * (b // 2):P * (b // 2) + P], p2[0:32, Q_BD + 512 * (b % 2):Q_BD + 512 * (b % 2) + 512], start=True, stop=True)
            ins.then_inc(g.pe2, 1)
            pe.wait_ge(g.dve2, DVE2["m_go"] + 1)
            pe.wait_ge(g.m_bg, 16)
            items = pe.value_load(item_i[0:1, 63:64], min_val=N_EXPERTS, max_val=N_EXPERTS + 16)

            def gather(value):
                pe.wait_ge(g.m_p, value)
                for k in range(KC):
                    for t in range(TT):
                        ins = pe.matmul(PS[:, 3, 64 * k:64 * k + 64], xn[:, t, P * k:P * k + P], hot1[:, t, 0:64], start=t == 0, stop=t == 1)
                ins.then_inc(g.m_xg, 1)

            def turn_hot():
                for t in range(TT):
                    ins = pe.transpose(PS[:, 5, P * t:P * t + P], hotw[:, t, :], ident)
                ins.then_inc(g.m_pw, 1)

            gather(1)
            turn_hot()
            with pe.Fori(0, items) as n:
                pe.wait_ge(g.m_xge, n + 1)
                for s in range(4):
                    pe.wait_ge(landed[s], (n + LOADS_BEFORE[s]) * 16 + 16)
                    for kk in range(2):
                        k = 2 * s + kk
                        for b in range(2):
                            for h in range(2):
                                o = 2048 * kk + 1024 * b + 512 * h
                                ins = pe.matmul(PS[64 * h:64 * h + 64, b, :], xg[:, 64 * k:64 * k + 64], ring[:, s, o:o + 512],
                                                start=k == 0, stop=False, skip_group_check=True)
                    ins.then_inc(freed[s], 1)
                pe.wait_ge(g.m_es, n + 1)
                for b in range(2):
                    for h in range(2):
                        o = 1024 * b + 512 * h
                        ins = pe.matmul(PS[64 * h:64 * h + 64, b, :], esel, bgu[:, o:o + 512], start=False, stop=True, skip_group_check=True)
                ins.then_inc(g.m_gu, 1)
                pe.wait_ge(g.m_sd, 2 * n + 1)
                gather(n + 2)
                pe.wait_ge(g.m_pwe, n + 1)
                turn_hot()
                pe.wait_ge(g.m_a, n + 1)
                for c in range(4):
                    ins = pe.transpose(PS[:, 4, P * c:P * c + P], mus[:, P * c:P * c + P], ident)
                ins.then_inc(g.m_at, 1)
                pe.wait_ge(g.m_ate, n + 1)
                for c in range(KC):
                    s = 4 + c // 4
                    if c % 4 == 0:
                        pe.wait_ge(landed[s], (n + LOADS_BEFORE[s]) * 16 + 16)
                    for h in range(2):
                        o = 1024 * (c % 4) + 512 * h
                        ins = pe.matmul(PS[64 * h:64 * h + 64, 2, :], aT[:, P * (c % 4) + 64 * (c // 4):P * (c % 4) + 64 * (c // 4) + 64],
                                        ring[:, s, o:o + 512], start=c == 0, stop=c == KC - 1, skip_group_check=True)
                    if c == 3:
                        ins.then_inc(freed[s], 1)
                ins.then_inc(g.m_y, 1)
                pe.wait_ge(g.m_y, n + 1)
                pe.sem_inc(freed[5], 1)
                pe.wait_ge(g.m_ye, n + 1)
                for t in range(TT):
                    for h in range(2):
                        rows = slice(64 * h, 64 * h + 64)
                        ins = pe.matmul(PS[:, (6 + h, 3 + h)[t], :], pwT[rows, P * t:P * t + P], ysb[rows, :], start=True, stop=True)
                    ins.then_inc(g.m_s, 1)

        @block.gpsimd
        def _(pool):
            link = Link(pool, g.u_pl)
            pool.wait_ge(g.r_ada, 3)
            pool.wait_ge(g.dve2, DVE2["u_cs"] + 1)

            def table(q):
                er, ei = (etab3[q % 3][:, i, :].rearrange("p (j t) -> p j t", j=4) for i in range(2))
                cos, sin = (s5v[:, c][:, 4 * q:4 * q + 4].unsqueeze(2) for c in (COS_, SIN_))
                link(pool.memset(er[:, :, 0:1], 1.0))
                link(pool.memset(ei[:, :, 0:1], 0.0))
                link(pool.tensor_copy(er[:, :, 1:2], cos))
                link(pool.tensor_copy(ei[:, :, 1:2], sin))
                w = 2
                while w < T:
                    c1, s1 = (m[:, :, w - 1:w] for m in (er, ei))
                    pw = ph.rearrange("p (i j) -> p i j", i=4).unsqueeze(3)
                    link(pool.tensor_tensor(pw[:, 0], c1, cos, ALU.mult))
                    link(pool.tensor_tensor(pw[:, 1], s1, sin, ALU.mult))
                    link(pool.tensor_tensor(pw[:, 2], c1, sin, ALU.mult))
                    link(pool.tensor_tensor(pw[:, 3], s1, cos, ALU.mult))
                    link(pool.tensor_tensor(pw[:, 0], pw[:, 0], pw[:, 1], ALU.subtract))
                    link(pool.tensor_tensor(pw[:, 2], pw[:, 2], pw[:, 3], ALU.add))
                    cw = pw[:, 0].broadcast_to([P, 4, w])
                    sw = pw[:, 2].broadcast_to([P, 4, w])
                    a0, b0, a1, b1 = er[:, :, 0:w], ei[:, :, 0:w], er[:, :, w:2 * w], ei[:, :, w:2 * w]
                    aux = paux[:, 0:4 * w].rearrange("p (j t) -> p j t", j=4)
                    link(pool.tensor_tensor(a1, a0, cw, ALU.mult))
                    link(pool.tensor_tensor(aux, b0, sw, ALU.mult))
                    link(pool.tensor_tensor(a1, a1, aux, ALU.subtract))
                    link(pool.tensor_tensor(b1, b0, cw, ALU.mult))
                    link(pool.tensor_tensor(aux, a0, sw, ALU.mult))
                    ins = pool.tensor_tensor(b1, b1, aux, ALU.add)
                    w *= 2
                    if w < T:
                        link(ins)
                    else:
                        link.to(ins, g.u_e, q + 1)

            table(0)
            table(1)
            pool.wait_ge(g.dve2, DVE2["r_mc"] + 1)
            table(2)
            pool.wait_ge(g.u_pd, 1)
            table(3)


def layouts(i):
    f = {n: np.asarray(v) for n, v in i.items()}
    a = {"x": f["x"], "rel_bias": f["rel_bias"]}
    k = shape_constants()
    a["constants"] = k
    a["buckets"] = bucket_constants()

    def rows_first(w, n):
        nl, d_in, d_out = w.shape
        return np.ascontiguousarray(w.reshape(nl, d_in // P, P, d_out // n, n).transpose(0, 3, 2, 1, 4)).reshape(nl, d_out // n, P, -1)

    full = 512 * (WIN_BLOCKS - 1)
    a["w_in_blocks"] = rows_first(f["w_in"][:, :, :full], 512)
    a["w_in_last"] = rows_first(f["w_in"][:, :, full:], WIN_LAST)[:, 0]
    a["w_out"] = rows_first(f["w_out"], 512)
    gu = f["w_gate_up"].reshape(DEPTH, D, 2, FF_BLOCKS, 256).transpose(0, 1, 3, 2, 4).reshape(DEPTH, D, FF_BLOCKS * 512)
    a["w_gate_up"] = rows_first(gu, 512)
    a["w_down"] = np.ascontiguousarray(f["w_down"].reshape(DEPTH, FF_TILES, P, D).transpose(0, 2, 1, 3)).reshape(DEPTH, P, FF_TILES * D)
    a["cmp_w1"] = np.ascontiguousarray(f["cmp_w1"].reshape(DEPTH, 2, 2, 16, HD, HD).transpose(0, 2, 4, 1, 3, 5)).reshape(DEPTH, P, 2048)
    lp = np.zeros((DEPTH, P, PC_N), np.float32)
    lp[:, :, PC_ATTN:PC_ATTN + 8] = f["attn_norm"].reshape(DEPTH, KC, P).transpose(0, 2, 1)
    lp[:, :, PC_FFN:PC_FFN + 8] = f["ffn_norm"].reshape(DEPTH, KC, P).transpose(0, 2, 1)
    for half in range(2):
        rows = slice(64 * half, 64 * half + 64)
        lp[:, rows, PC_QG] = f["nsa_q_gain"]
        lp[:, rows, PC_KG:PC_KG + 3] = f["nsa_k_gain"].transpose(0, 2, 1)
        pe = f["cmp_pe"][:, :, 16 * half:16 * half + 16, :]
        lp[:, rows, PC_PE:PC_PE + 32] = pe.transpose(0, 3, 1, 2).reshape(DEPTH, 64, 32)
    lp[:, :, PC_GB:PC_GB + 4] = f["gm_b"].transpose(0, 2, 1)
    lp[:, :, PC_WS:PC_WS + 512] = f["gm_ws"].transpose(0, 3, 1, 2).reshape(DEPTH, P, 512)
    lp[:, 0:64, PC_W2:PC_W2 + 128] = f["cmp_w2"].transpose(0, 2, 1, 3).reshape(DEPTH, 64, 128)
    a["layer_params"] = lp

    ada = f["ada_w_2"][0]
    a["ada_w"] = rows_first(ada[None], 512)[0]
    w2 = f["w_in_2"][0]
    cols = np.concatenate([w2[:, 1552:2064], w2[:, 0:1536]], axis=1)
    a["w_in_2"] = rows_first(cols[None], 512)[0]
    a["s5_glu_w"] = np.ascontiguousarray(f["s5_glu_w_2"][0].reshape(4, P, 512).transpose(1, 0, 2)).reshape(P, 2048)
    a["w_out_2"] = rows_first(f["w_out_2"], 512)[0]
    a["exp_w_gu"], a["exp_w_down"], a["exp_b_gu"] = f["exp_w_gu_2"][0], f["exp_w_down_2"][0], f["exp_b_gu_2"][0]
    a["ada_b_gates"] = np.concatenate([f["ada_b_2"][:, 2048:3072], f["ada_b_2"][:, 5120:6144]], axis=1)
    a["post_gains"] = np.concatenate([f["mix_post_g_2"], f["ffn_post_g_2"]], axis=1)
    a["gla_norm_g"] = f["gla_norm_g_2"]
    q = np.zeros((P, Q_N), np.float32)

    def column(at, v):
        q[:, at:at + v.size // P] = v.reshape(-1, P).T

    column(Q_MPRE, f["mix_pre_g_2"])
    column(Q_FPRE, f["ffn_pre_g_2"])
    column(Q_ADB, f["ada_b_2"])
    column(Q_BAL, f["b_alpha_2"])
    column(Q_LRE, f["s5_lambda_re_2"])
    column(Q_LIM, f["s5_lambda_im_2"])
    column(Q_LDT, np.repeat(f["s5_log_dt_2"][0], 64))
    column(Q_D, f["s5_d_2"])
    column(Q_GLB, f["s5_glu_b_2"])
    q[0:16, Q_WA:Q_WA + 256] = f["w_alpha_2"][0]
    q[:, Q_WL:Q_WL + 128] = w2[:, 1536:1552].reshape(KC, P, 16).transpose(1, 0, 2).reshape(P, 128)
    q[:, Q_RW:Q_RW + 256] = f["router_w_2"][0].reshape(KC, P, 32).transpose(1, 0, 2).reshape(P, 256)
    column(Q_C, f["c_2"])
    q[:, Q_RB:Q_RB + 32] = f["router_b_2"]
    q[0:32, Q_BD:Q_BD + 1024] = f["exp_b_down_2"][0]
    a["params_2"] = q
    m = np.zeros((4, P, 4, P), np.float32)
    for g in range(32):
        tile, rows, half = g // 8, 16 * (g % 8), 64 * (g % 2)
        for i, b in enumerate(("s5_b_re_2", "s5_b_im_2")):
            m[i, rows:rows + 16, tile, half:half + 64] = f[b][0, g].T
        for i, c in enumerate(("s5_c_re_2", "s5_c_im_2")):
            m[2 + i, half:half + 64, tile, rows:rows + 16] = f[c][0, g].T
    a["ssm_matrices"] = np.ascontiguousarray(m.transpose(1, 0, 2, 3)).reshape(P, 2048)
    return a


def kernel(**inputs):
    import concourse.bacc as bacc
    from concourse.bass_utils import run_bass_kernel_spmd as run

    nc = bacc.Bacc("TRN2", target_bir_lowering=False, num_devices=1)
    arrays = {"in_" + n: np.ascontiguousarray(v) for n, v in layouts(inputs).items()}
    a = {n[3:]: nc.dram_tensor(n, v.shape, mybir.dt.from_np(v.dtype), kind="ExternalInput").ap() for n, v in arrays.items()}
    out = nc.dram_tensor("out", (1, T, D), F32, kind="ExternalOutput").ap()
    scratch = nc.dram_tensor("bias_rows", (NH, 512), F32, kind="Internal").ap()
    program(nc, a, out, scratch)
    return run(nc, [arrays], core_ids=[0]).results[0]["out"]
```
